# Optimizing a Trainium2 kernel written in Bass

```python
import jax, jax.numpy as jnp
from jax import lax
import numpy as np

D_MODEL = 1024
BATCH = 1
SEQ = 1024
DEPTH = 1

GRID_W = 64
EPS = 1e-6
SSD_HEADS = 16
SSD_HEADDIM = 64
D_SSD = SSD_HEADS * SSD_HEADDIM
SSD_GROUPS = 4
SSD_HPG = SSD_HEADS // SSD_GROUPS
SSD_STATE = 128
SSD_CHUNK = 128
CONV_W = 5
D_XBC = D_SSD + 2 * SSD_GROUPS * SSD_STATE
NA_HEADS = 16
NA_HEADDIM = 64
D_NA = NA_HEADS * NA_HEADDIM
NA_KH = 8
NA_KW = 16
NA_QB = 16
NA_KB = NA_QB + NA_KW
PEER_HEADS = 8
PEER_NKEYS = 128
PEER_EXPERTS = PEER_NKEYS * PEER_NKEYS
PEER_TOPK = 16
PEER_DKEY = 256
PEER_DHALF = PEER_DKEY // 2
PEER_CHUNK = 128
IN_SIZES = (D_SSD, D_XBC, SSD_HEADS, SSD_HEADS, 3 * D_NA, D_MODEL, D_MODEL)
D_IN = sum(IN_SIZES)
IN_OFFSETS = [int(o) for o in np.cumsum(IN_SIZES)[:-1]]

kernel_name = "hybrid_ssd_natten_peer_block"

def rms_norm(x, g):
    xf = x.astype(jnp.float32)
    y = xf * lax.rsqrt(jnp.mean(xf * xf, axis=-1, keepdims=True) + EPS)
    return (y * g.astype(jnp.float32)).astype(x.dtype)

def modulate(h, g, shift, scale):
    return rms_norm(h, g) * (1 + scale[:, None, :]) + shift[:, None, :]

def ssd_direction(xh, dt, a, bm, cm):
    b, l, g, k, p = xh.shape
    nc, L = l // SSD_CHUNK, SSD_CHUNK
    f32 = jnp.float32
    xdt = (xh.astype(f32) * dt[..., None]).reshape(b, nc, L, g, k, p)
    bc = bm.astype(f32).reshape(b, nc, L, g, SSD_STATE)
    cc = cm.astype(f32).reshape(b, nc, L, g, SSD_STATE)
    da = (dt * a).reshape(b, nc, L, g, k).transpose(0, 3, 4, 1, 2)
    cs = jnp.cumsum(da, axis=-1)
    lower = jnp.tril(jnp.ones((L, L), dtype=bool))
    seg = jnp.exp(jnp.where(lower, cs[..., :, None] - cs[..., None, :], -jnp.inf))
    cb = jnp.einsum('bclgn,bcsgn->bcgls', cc, bc)
    y_diag = jnp.einsum('bcgls,bgkcls,bcsgkp->bclgkp', cb, seg, xdt)
    decay_in = jnp.exp(cs[..., -1:] - cs)
    states = jnp.einsum('bclgn,bgkcl,bclgkp->cbgkpn', bc, decay_in, xdt)
    chunk_decay = jnp.exp(cs[..., -1]).transpose(3, 0, 1, 2)

    def step(hs, inp):
        s_c, d_c = inp
        return d_c[..., None, None] * hs + s_c, hs

    _, prev = lax.scan(step, jnp.zeros(states.shape[1:], f32), (states, chunk_decay))
    y_off = jnp.einsum('bclgn,cbgkpn,bgkcl->bclgkp', cc, prev, jnp.exp(cs))
    return (y_diag + y_off).reshape(b, l, g, k, p)

def ssd_branch(z, xbc, dt_raw_f, dt_raw_b, conv_w, conv_b, dt_bias_f, dt_bias_b,
               a_log_f, a_log_b, d_skip, norm_g):
    b, l, _ = xbc.shape
    f32 = jnp.float32
    xbc = lax.conv_general_dilated(xbc, conv_w[:, None, :].astype(xbc.dtype), (1,),
                                   [(CONV_W // 2, CONV_W // 2)],
                                   dimension_numbers=('NWC', 'WIO', 'NWC'),
                                   feature_group_count=D_XBC)
    xbc = jax.nn.silu(xbc + conv_b)
    xs, bm, cm = jnp.split(xbc, [D_SSD, D_SSD + SSD_GROUPS * SSD_STATE], axis=-1)
    xh = xs.reshape(b, l, SSD_GROUPS, SSD_HPG, SSD_HEADDIM)
    bm = bm.reshape(b, l, SSD_GROUPS, SSD_STATE)
    cm = cm.reshape(b, l, SSD_GROUPS, SSD_STATE)
    gk = (b, l, SSD_GROUPS, SSD_HPG)
    dt_f = jax.nn.softplus(dt_raw_f.astype(f32) + dt_bias_f.astype(f32)).reshape(gk)
    dt_b = jax.nn.softplus(dt_raw_b.astype(f32) + dt_bias_b.astype(f32)).reshape(gk)
    a_f = -jnp.exp(a_log_f.astype(f32)).reshape(SSD_GROUPS, SSD_HPG)
    a_b = -jnp.exp(a_log_b.astype(f32)).reshape(SSD_GROUPS, SSD_HPG)
    y_f = ssd_direction(xh, dt_f, a_f, bm, cm)
    y_b = ssd_direction(xh[:, ::-1], dt_b[:, ::-1], a_b, bm[:, ::-1], cm[:, ::-1])[:, ::-1]
    y = y_f + y_b + d_skip.astype(f32).reshape(SSD_GROUPS, SSD_HPG, 1) * xh.astype(f32)
    y = y.reshape(b, l, D_SSD).astype(z.dtype)
    return rms_norm(y * jax.nn.silu(z), norm_g)

def neighbourhood_attention(q, k, v, rpb):
    b, l, _ = q.shape
    rows = l // GRID_W
    kh = min(NA_KH, rows)
    ncb = GRID_W // NA_QB

    def grid(t):
        return t.reshape(b, rows, GRID_W, NA_HEADS, NA_HEADDIM).transpose(0, 3, 1, 2, 4)

    qg = grid(q) * (NA_HEADDIM ** -0.5)
    kg, vg = grid(k), grid(v)
    cols = np.arange(GRID_W)
    win_start = np.clip(cols - NA_KW // 2, 0, GRID_W - NA_KW).reshape(ncb, NA_QB)
    blk_start = np.clip(np.arange(ncb) * NA_QB - NA_KW // 2, 0, GRID_W - NA_KB)
    key_cols = blk_start[:, None] + np.arange(NA_KB)
    q_cols = cols.reshape(ncb, NA_QB)
    kc = key_cols[:, None, :]
    in_win = (kc >= win_start[:, :, None]) & (kc < win_start[:, :, None] + NA_KW)
    dcol = np.clip(kc - q_cols[:, :, None] + NA_KW - 1, 0, 2 * NA_KW - 2)
    col_bias = jnp.where(in_win, rpb.astype(jnp.float32)[:, :, dcol], -jnp.inf)

    def row(r):
        rs = jnp.clip(r - kh // 2, 0, rows - kh)
        drow = rs + jnp.arange(kh) - r + NA_KH - 1
        bias = col_bias[:, drow].transpose(0, 2, 3, 1, 4)
        qr = lax.dynamic_index_in_dim(qg, r, axis=2, keepdims=False)
        qr = qr.reshape(b, NA_HEADS, ncb, NA_QB, NA_HEADDIM)
        kr = lax.dynamic_slice_in_dim(kg, rs, kh, axis=2)[:, :, :, key_cols]
        vr = lax.dynamic_slice_in_dim(vg, rs, kh, axis=2)[:, :, :, key_cols]
        s = jnp.einsum('bhmqd,bhimjd->bhmqij', qr, kr).astype(jnp.float32) + bias
        sh = s.shape
        p = jax.nn.softmax(s.reshape(sh[0], sh[1], sh[2], sh[3], kh * NA_KB), axis=-1)
        p = p.reshape(sh).astype(vr.dtype)
        o = jnp.einsum('bhmqij,bhimjd->bhmqd', p, vr)
        return o.reshape(b, NA_HEADS, GRID_W, NA_HEADDIM)

    out = lax.map(row, jnp.arange(rows))
    return out.transpose(1, 0, 3, 2, 4).reshape(b, l, D_NA)

def peer(xn, w_q, sub_keys, u, v):
    b, l, d = xn.shape
    xt = xn.reshape(-1, PEER_CHUNK, d)

    def chunk(xc):
        q = (xc @ w_q).reshape(PEER_CHUNK, PEER_HEADS, 2, PEER_DHALF)
        s = jnp.einsum('thzd,znd->thzn', q, sub_keys).astype(jnp.float32)
        s1, i1 = lax.top_k(s[:, :, 0], PEER_TOPK)
        s2, i2 = lax.top_k(s[:, :, 1], PEER_TOPK)
        cand = (s1[..., :, None] + s2[..., None, :]).reshape(PEER_CHUNK, PEER_HEADS, PEER_TOPK * PEER_TOPK)
        cidx = (i1[..., :, None] * PEER_NKEYS + i2[..., None, :]).reshape(PEER_CHUNK, PEER_HEADS, PEER_TOPK * PEER_TOPK)
        top, pos = lax.top_k(cand, PEER_TOPK)
        eidx = jnp.take_along_axis(cidx, pos, axis=-1)
        gate = jax.nn.softmax(top, axis=-1)
        act = jax.nn.gelu(jnp.einsum('thkd,td->thk', u[eidx], xc).astype(jnp.float32), approximate=False)
        return jnp.einsum('thk,thkd->td', (gate * act).astype(v.dtype), v[eidx])

    return lax.map(chunk, xt).reshape(b, l, d)

def hybrid_layer(h, c, w_ada, b_ada, norm1_g, w_in, conv_w, conv_b, dt_bias_f, dt_bias_b,
                 a_log_f, a_log_b, d_skip, ssd_norm_g, w_ssd_br, na_rpb, w_na_br, w_out,
                 norm2_g, peer_wq, peer_keys, peer_u, peer_v):
    mod = jax.nn.silu(c) @ w_ada + b_ada
    sh1, sc1, g1, sh2, sc2, g2 = jnp.split(mod, 6, axis=-1)
    n1 = modulate(h, norm1_g, sh1, sc1)
    proj = n1 @ w_in
    z, xbc, dtf, dtb, qkv, gate_ssd, gate_na = jnp.split(proj, IN_OFFSETS, axis=-1)
    y_ssd = ssd_branch(z, xbc, dtf, dtb, conv_w, conv_b, dt_bias_f, dt_bias_b,
                       a_log_f, a_log_b, d_skip, ssd_norm_g) @ w_ssd_br
    q, k, v = jnp.split(qkv, 3, axis=-1)
    y_na = neighbourhood_attention(q, k, v, na_rpb) @ w_na_br
    mixed = jax.nn.sigmoid(gate_ssd) * y_ssd + jax.nn.sigmoid(gate_na) * y_na
    h = h + g1[:, None, :] * (mixed @ w_out)
    n2 = modulate(h, norm2_g, sh2, sc2)
    h = h + g2[:, None, :] * peer(n2, peer_wq, peer_keys, peer_u, peer_v)
    return h

def setup_inputs(seed: int = 0) -> dict:
    key = jax.random.key(seed)
    ks = jax.random.split(key, 32)
    f32 = jnp.float32
    nrm = lambda k, shape, s: jax.random.normal(k, shape, f32) * s
    dt0 = jnp.exp(jax.random.uniform(ks[8], (DEPTH, 2, SSD_HEADS), f32) * (np.log(0.1) - np.log(0.001)) + np.log(0.001))
    dt_bias = dt0 + jnp.log(-jnp.expm1(-dt0))
    a_log = jnp.log(jax.random.uniform(ks[9], (DEPTH, 2, SSD_HEADS), f32, 1.0, 16.0))
    return {
        "x": nrm(ks[0], (BATCH, SEQ, D_MODEL), 1.0),
        "c": nrm(ks[1], (BATCH, D_MODEL), 1.0),
        "w_ada": nrm(ks[2], (DEPTH, D_MODEL, 6 * D_MODEL), D_MODEL ** -0.5),
        "b_ada": nrm(ks[3], (DEPTH, 6 * D_MODEL), 0.01),
        "norm1_g": 1.0 + nrm(ks[4], (DEPTH, D_MODEL), 0.05),
        "w_in": nrm(ks[5], (DEPTH, D_MODEL, D_IN), D_MODEL ** -0.5),
        "conv_w": nrm(ks[6], (DEPTH, CONV_W, D_XBC), CONV_W ** -0.5),
        "conv_b": nrm(ks[7], (DEPTH, D_XBC), 0.01),
        "dt_bias_f": dt_bias[:, 0],
        "dt_bias_b": dt_bias[:, 1],
        "a_log_f": a_log[:, 0],
        "a_log_b": a_log[:, 1],
        "d_skip": 1.0 + nrm(ks[10], (DEPTH, SSD_HEADS), 0.1),
        "ssd_norm_g": 1.0 + nrm(ks[11], (DEPTH, D_SSD), 0.05),
        "w_ssd_br": nrm(ks[12], (DEPTH, D_SSD, D_MODEL), D_SSD ** -0.5),
        "na_rpb": nrm(ks[13], (DEPTH, NA_HEADS, 2 * NA_KH - 1, 2 * NA_KW - 1), 0.1),
        "w_na_br": nrm(ks[14], (DEPTH, D_NA, D_MODEL), D_NA ** -0.5),
        "w_out": nrm(ks[15], (DEPTH, D_MODEL, D_MODEL), D_MODEL ** -0.5),
        "norm2_g": 1.0 + nrm(ks[16], (DEPTH, D_MODEL), 0.05),
        "peer_wq": nrm(ks[17], (DEPTH, D_MODEL, PEER_HEADS * PEER_DKEY), D_MODEL ** -0.5),
        "peer_keys": nrm(ks[18], (DEPTH, 2, PEER_NKEYS, PEER_DHALF), PEER_DHALF ** -0.5),
        "peer_u": nrm(ks[19], (DEPTH, PEER_EXPERTS, D_MODEL), D_MODEL ** -0.5),
        "peer_v": nrm(ks[20], (DEPTH, PEER_EXPERTS, D_MODEL), PEER_HEADS ** -0.5),
        "final_g": 1.0 + nrm(ks[21], (D_MODEL,), 0.05),
    }

def reference(x, c, w_ada, b_ada, norm1_g, w_in, conv_w, conv_b, dt_bias_f, dt_bias_b,
              a_log_f, a_log_b, d_skip, ssd_norm_g, w_ssd_br, na_rpb, w_na_br, w_out,
              norm2_g, peer_wq, peer_keys, peer_u, peer_v, final_g):
    h = x
    for i in range(DEPTH):
        h = hybrid_layer(h, c, w_ada[i], b_ada[i], norm1_g[i], w_in[i], conv_w[i], conv_b[i],
                         dt_bias_f[i], dt_bias_b[i], a_log_f[i], a_log_b[i], d_skip[i],
                         ssd_norm_g[i], w_ssd_br[i], na_rpb[i], w_na_br[i], w_out[i],
                         norm2_g[i], peer_wq[i], peer_keys[i], peer_u[i], peer_v[i])
    return rms_norm(h, final_g)


_drawn_inputs = setup_inputs


def setup_inputs(seed=0):
    import zlib

    import numpy as np

    out = dict(_drawn_inputs(seed))
    spreads = {}
    factors = {'b_ada': 3.12, 'conv_b': 6.682, 'd_skip': 4.704, 'ssd_norm_g': 2.842, 'na_rpb': 4.343}
    for name, (base, spread) in spreads.items():
        noise = np.random.default_rng([zlib.crc32(name.encode()), seed]).standard_normal(out[name].shape)
        drawn = base * np.exp(spread * noise) if base else spread * noise
        out[name] = __import__('jax').numpy.asarray(drawn.astype(out[name].dtype))
    for name, factor in factors.items():
        out[name] = (out[name] * factor).astype(out[name].dtype)
    return out
```

```python
import numpy as np
import concourse.bass as bass
from concourse import mybir
from contextlib import ExitStack

P = 128
SEQ, DM = 1024, 1024
TT = SEQ // P
KD = DM // P
HALF = 512
GRID_W, GRID_H = 64, SEQ // 64
EPS = 1e-6
SSD_HEADS, HEADDIM, GROUPS, HPG, STATE = 16, 64, 4, 4, 128
CONV_W = 5
D_XBC = DM + 2 * GROUPS * STATE
XBC_BLOCKS = D_XBC // P
NA_HEADS, NA_KH, NA_KW = 16, 8, 16
PAIRS = NA_HEADS // 2
COL_Z, COL_XBC = 0, DM
COL_DT = COL_XBC + D_XBC
COL_QKV = COL_DT + 2 * SSD_HEADS
COL_GATES = COL_QKV + 3 * DM
MODS = 6 * DM
BIAS_ROWS, BIAS_COLS = 17, 128
BIAS_PAD = 48
SLOTS = 16
MASKED = -1.0e30
PEER_HEADS, NKEYS, TOPK, DHALF = 8, 128, 16, 128
QW = PEER_HEADS * 2 * DHALF
PICKS = PEER_HEADS * TOPK
LOWEST = -3.0e38


def build_program(nc, a, out):
    f32, u32 = mybir.dt.float32, mybir.dt.uint32
    ALU, ACT, AX = mybir.AluOpType, mybir.ActivationFunctionType, mybir.AxisListType

    def scratch(name, shape):
        return nc.dram_tensor(name, shape, f32).ap()

    mod_scr = scratch("mod_scr", [MODS])
    rpb_scr = scratch("rpb_scr", [NA_HEADS, BIAS_ROWS, GRID_W, GRID_W])
    zg_scr = scratch("zg_scr", [3, SEQ, DM])
    na_scr = scratch("na_scr", [SEQ, DM])
    mix_scr = scratch("mix_scr", [SEQ, DM])
    w_in = a["w_in"][0].rearrange("(k p) n -> p k n", p=P)

    top = ExitStack()
    with top:
        def opener(ctx):
            def sb(name, shape, dt=f32):
                return ctx.enter_context(nc.sbuf_tensor(name, shape, dt))
            return sb

        def banks(ctx, name, n):
            return ctx.enter_context(nc.psum_tensor(name, [P, n * HALF], f32))

        stored = nc.alloc_semaphore(name="out_stored")
        held = []

        def sem(name):
            held.append(nc.alloc_semaphore(name=name))
            return held[-1]

        def retire_semaphores():
            nc.clear_and_free_semaphores(held)
            nc.all_engine_barrier()
            held.clear()

        sb = opener(top)
        ident = sb("ident", [P, P])

        mid = ExitStack()
        with mid:
            sbm = opener(mid)
            upto = sbm("upto", [P, P])
            since = sbm("since", [P, P])
            after = sbm("after", [P, P])
            before = sbm("before", [P, P])
            ones = sbm("ones", [P, P])
            X = sbm("X", [P, TT, DM])
            y_rstd = sbm("y_rstd", [P, TT])
            scan = ExitStack()
            with scan:
                sbs = opener(scan)
                BT = sbs("BT", [P, GROUPS, SEQ])
                CT = sbs("CT", [P, GROUPS, SEQ])
                dt = sbs("dt", [P, TT, 2 * SSD_HEADS])
                dA = sbs("dA", [P, TT, 2 * SSD_HEADS])
                front = ExitStack()
                with front:
                    n1T = opener(front)("n1T", [P, KD, SEQ])
                    consts = (ident, upto, since, after, before, ones)
                    stage_condition(nc, a, opener, banks, sem, consts, X, n1T, mod_scr, rpb_scr)
                    stage_project(nc, a, opener, banks, sem, w_in, ident, n1T, X, BT, CT, dt, dA, zg_scr)
                    stage_attention(nc, a, opener, banks, sem, w_in, ident, n1T, rpb_scr, na_scr)
                retire_semaphores()
                stage_ssd(nc, a, opener, banks, sem, consts, X, BT, CT, dt, dA, zg_scr, y_rstd)
            stage_merge(nc, a, opener, banks, sem, ident, X, y_rstd, zg_scr, na_scr, mix_scr)
        retire_semaphores()
        stage_peer(nc, a, opener, banks, sem, ident, mod_scr, mix_scr, out, stored)


def stage_condition(nc, a, opener, banks, sem, consts, xs, n1T, mod_scr, rpb_scr):
    f32 = mybir.dt.float32
    ALU, ACT = mybir.AluOpType, mybir.ActivationFunctionType
    ident, upto, since, after, before, ones = consts
    CH = MODS // 6
    NCH = 6
    CB = CH // P
    ctx = ExitStack()
    with ctx:
        sb = opener(ctx)
        c_rows = sb("c_rows", [KD, P])
        c_act = sb("c_act", [KD, P])
        cT = sb("cT", [P, KD])
        b_ada = sb("b_ada", [16, 3, P])
        ada = sb("ada", [P, 2, KD, CH])
        mod_cols = sb("mod_cols", [P, 48])
        mod_rows = sb("mod_rows", [16, 3, P])
        shift = sb("shift", [P, DM])
        scale = sb("scale", [P, DM])
        gain = sb("gain", [P, DM])
        junk = sb("junkA", [P, DM])
        sumsq = sb("sumsqA", [P, TT])
        rstd = sb("rstdA", [P, TT])
        bias_pad = sb("bias_pad", [NA_HEADS, BIAS_ROWS, BIAS_COLS])
        ps_c = banks(ctx, "ps_c", 1)
        ps_mod = banks(ctx, "ps_mod", 1)
        ps_row = banks(ctx, "ps_row", 1)
        ps_n = [banks(ctx, f"ps_n{i}", 2) for i in range(2)]

        s_small, s_x, s_gain = sem("a_small"), sem("a_x"), sem("a_gain")
        s_ada = [sem("a_ada0"), sem("a_ada1")]
        s_modw, s_modr, s_pad, s_padw = sem("a_modw"), sem("a_modr"), sem("a_pad"), sem("a_padw")
        c_done, cps_done, cT_done = sem("a_c"), sem("a_cps"), sem("a_cT")
        mm_done, cols_done, rows_ps, rows_done = sem("a_mm"), sem("a_cols"), sem("a_rowsps"), sem("a_rows")
        const_zero, const_done, pad_zero = sem("a_cz"), sem("a_cd"), sem("a_pz")
        sq_done, sqrt_done, chain, n_done, tr_done, ev_done = (
            sem("a_sq"), sem("a_sqrt"), sem("a_chain"), sem("a_n"), sem("a_tr"), sem("a_ev"))

        with nc.Block() as block:
            @block.sync
            def _(sp):
                sp.dma_start(c_rows[:, :], a["c"].rearrange("a (k p) -> (a k) p", p=P)).then_inc(s_small, 16)
                sp.dma_start(b_ada[:, :, :], a["b_ada"][0].rearrange("(g r p) -> r g p", p=P, r=16)).then_inc(s_small, 16)
                w_ada = a["w_ada"][0].rearrange("(k p) n -> p k n", p=P)

                def load(q):
                    sp.dma_start(ada[:, q % 2, :, :], w_ada[:, :, q * CH:(q + 1) * CH]).then_inc(s_ada[q % 2], 16)

                load(0)
                load(1)
                sp.dma_start(xs[:, :, :], a["x"][0].rearrange("(t p) d -> p t d", p=P)).then_inc(s_x, 16)
                sp.dma_start(gain[:, :], a["norm1_g"][0].partition_broadcast(P)).then_inc(s_gain, 16)
                sp.wait_ge(pad_zero, 1)
                sp.dma_start(bias_pad[:, 1:16, BIAS_PAD:BIAS_PAD + 31], a["na_rpb"][0]).then_inc(s_pad, 16)
                sp.wait_ge(s_pad, 16)
                for r in range(BIAS_ROWS):
                    whole = bias_pad[:, r, :]
                    skewed = bass.AP(whole.tensor, whole.offset + BIAS_PAD + NA_KW - 1, [list(whole.ap[0]), [-1, GRID_W], [1, GRID_W]])
                    sp.dma_start(rpb_scr[:, r, :, :], skewed).then_inc(s_padw, 16)
                for q in (2, 3):
                    sp.wait_ge(mm_done, q - 1)
                    load(q)
                sp.wait_ge(rows_done, 1)
                sp.dma_start(mod_scr[0:2 * DM].rearrange("(r p) -> r p", p=P), mod_rows[:, 0, :]).then_inc(s_modw, 16)
                sp.wait_ge(s_modw, 16)
                sp.dma_start(shift[:, :], mod_scr[0:DM].partition_broadcast(P)).then_inc(s_modr, 16)
                sp.dma_start(scale[:, :], mod_scr[DM:2 * DM].partition_broadcast(P)).then_inc(s_modr, 16)
                for q in (4, 5):
                    sp.wait_ge(mm_done, q - 1)
                    load(q)
                for g in (1, 2):
                    sp.wait_ge(rows_done, g + 1)
                    sp.dma_start(mod_scr[g * 2 * DM:(g + 1) * 2 * DM].rearrange("(r p) -> r p", p=P),
                                 mod_rows[:, g, :]).then_inc(s_modw, 16)
                sp.wait_ge(s_modw, 48)
                sp.wait_ge(s_padw, 16 * BIAS_ROWS)

            @block.gpsimd
            def _(pool):
                nc.gpsimd.memset(ident[:, :], 0.0).then_inc(const_zero, 1)
                for m in (upto, since, after, before):
                    nc.gpsimd.memset(m[:, :], 1.0).then_inc(const_zero, 1)
                pool.wait_ge(const_zero, 5)
                nc.gpsimd.affine_select(out=ident[:, :], in_=ident[:, :], compare_op=ALU.not_equal, fill=1.0,
                                        base=0, pattern=[[-1, P]], channel_multiplier=1).then_inc(const_done, 1)
                nc.gpsimd.memset(ones[:, :], 1.0)
                nc.gpsimd.memset(bias_pad[:, :, :], 0.0).then_inc(pad_zero, 1)
                for m, sign, op in ((upto, -1, ALU.is_ge), (since, 1, ALU.is_ge), (after, 1, ALU.is_gt), (before, -1, ALU.is_gt)):
                    nc.gpsimd.affine_select(out=m[:, :], in_=m[:, :], compare_op=op, fill=0.0, base=0,
                                            pattern=[[-sign, P]], channel_multiplier=sign).then_inc(const_done, 1)

            @block.scalar
            def _(act):
                act.wait_ge(s_small, 32)
                nc.scalar.activation(c_act[:, :], c_rows[:, :], ACT.Silu).then_inc(c_done, 1)
                act.wait_ge(cps_done, 1)
                nc.scalar.activation(cT[:, :], ps_c[:, 0:KD], ACT.Copy).then_inc(cT_done, 1)
                act.wait_ge(s_x, 16)
                for t in range(TT):
                    if t:
                        act.wait_ge(sq_done, t)
                    nc.scalar.activation(junk[:, :], xs[:, t, :], ACT.Square, accum_out=sumsq[:, t:t + 1]).then_inc(sq_done, 1)
                act.wait_ge(chain, 1)
                nc.scalar.activation(rstd[:, :], rstd[:, :], ACT.Sqrt).then_inc(sqrt_done, 1)
                for t in range(TT):
                    act.wait_ge(tr_done, t + 1)
                    nc.scalar.activation(n1T[:, :, t * P:(t + 1) * P],
                                         ps_n[t % 2][:, :].rearrange("p (k n) -> p k n", k=KD), ACT.Copy).then_inc(ev_done, 1)

            @block.vector
            def _(v):
                v.wait_ge(sq_done, TT)
                nc.vector.tensor_scalar(rstd[:, :], sumsq[:, :], 1.0 / DM, EPS, ALU.mult, ALU.add).then_inc(chain, 1)
                v.wait_ge(sqrt_done, 1)
                nc.vector.reciprocal(rstd[:, :], rstd[:, :]).then_inc(chain, 1)

                def rows(g):
                    v.wait_ge(mm_done, 2 * g + 2)
                    nc.vector.tensor_copy(mod_cols[:, g * 16:(g + 1) * 16], ps_mod[:, g * 16:(g + 1) * 16]).then_inc(cols_done, 1)
                    v.wait_ge(rows_ps, g + 1)
                    nc.vector.tensor_tensor(mod_rows[:, g, :], ps_row[0:16, 0:P], b_ada[:, g, :], ALU.add).then_inc(rows_done, 1)

                v.wait_ge(s_small, 32)
                rows(0)
                v.wait_ge(s_modr, 32)
                v.wait_ge(s_gain, 16)
                nc.vector.scalar_tensor_tensor(out=gain[:, :], in0=scale[:, :], scalar=1.0, in1=gain[:, :],
                                               op0=ALU.add, op1=ALU.mult).then_inc(chain, 1)
                v.wait_ge(chain, 3)
                for t in range(TT):
                    nc.vector.scalar_tensor_tensor(out=xs[:, t, :], in0=xs[:, t, :], scalar=rstd[:, t:t + 1], in1=gain[:, :],
                                                   op0=ALU.mult, op1=ALU.mult).then_inc(chain, 1)
                    v.wait_ge(chain, 4 + t)
                    nc.vector.tensor_tensor(xs[:, t, :], xs[:, t, :], shift[:, :], ALU.add).then_inc(n_done, 1)
                rows(1)
                rows(2)

            @block.tensor
            def _(pe):
                pe.wait_ge(const_done, 1)
                pe.wait_ge(c_done, 1)
                nc.tensor.transpose(ps_c[:, 0:KD], c_act[:, :], ident[0:KD, 0:KD]).then_inc(cps_done, 1)
                pe.wait_ge(cT_done, 1)

                def products(q):
                    pe.wait_ge(s_ada[q % 2], 16 * (q // 2 + 1))
                    if q in (2, 4):
                        pe.wait_ge(cols_done, q // 2)
                    for cb in range(CB):
                        for k in range(KD):
                            last = nc.tensor.matmul(ps_mod[:, q * CB + cb:q * CB + cb + 1],
                                                    ada[:, q % 2, k, cb * P:(cb + 1) * P], cT[:, k:k + 1],
                                                    start=(k == 0), stop=(k == KD - 1))
                    last.then_inc(mm_done, 1)

                def to_rows(g):
                    pe.wait_ge(cols_done, g + 1)
                    if g:
                        pe.wait_ge(rows_done, g)
                    nc.tensor.transpose(ps_row[0:16, 0:P], mod_cols[:, g * 16:(g + 1) * 16], ident[:, :]).then_inc(rows_ps, 1)

                products(0)
                products(1)
                to_rows(0)
                for t in range(TT):
                    pe.wait_ge(n_done, t + 1)
                    if t >= 2:
                        pe.wait_ge(ev_done, t - 1)
                    for k in range(KD):
                        last = nc.tensor.transpose(ps_n[t % 2][:, k * P:(k + 1) * P], xs[:, t, k * P:(k + 1) * P], ident[:, :])
                    last.then_inc(tr_done, 1)
                products(2)
                products(3)
                to_rows(1)
                products(4)
                products(5)
                to_rows(2)


def stage_project(nc, a, opener, banks, sem, w_in, ident, n1T, X, BT, CT, dt, dA, zg_scr):
    f32 = mybir.dt.float32
    ALU, ACT = mybir.AluOpType, mybir.ActivationFunctionType
    NH2 = 2 * SSD_HEADS
    ZB = 6
    z_cols = [COL_Z, COL_Z + HALF] + [COL_GATES + i * HALF for i in range(4)]
    RW, RZ, RS = 3, 2, 4
    ctx = ExitStack()
    with ctx:
        sb = opener(ctx)
        w_x = sb("w_x", [P, RW, KD, P])
        w_z = sb("w_z", [P, RZ, KD, HALF])
        w_dt = sb("w_dt", [P, KD, NH2])
        taps_rows = sb("taps_rows", [(CONV_W + 1) * XBC_BLOCKS, P])
        taps = sb("taps", [P, CONV_W + 1, XBC_BLOCKS])
        padded = sb("padded", [P, 2, SEQ + CONV_W - 1])
        conv = sb("conv", [P, 2, SEQ])
        xT = sb("xT", [P, 2, SEQ])
        staged = sb("staged", [P, RS, HALF])
        dt_bias = sb("dt_bias", [P, NH2])
        a_exp = sb("a_exp", [P, NH2])
        neg = sb("neg", [P, TT, NH2])
        ps_x = [banks(ctx, f"ps_x{i}", 2) for i in range(2)]
        ps_t = banks(ctx, "ps_t", 2)
        ps_dt = banks(ctx, "ps_dt", 1)

        s_small = sem("b_small")
        s_wx = [sem(f"b_wx{i}") for i in range(RW)]
        s_wz = [sem(f"b_wz{i}") for i in range(RZ)]
        s_st = [sem(f"b_st{i}") for i in range(RS)]
        taps_ps, taps_done, edge_done = sem("b_tapsps"), sem("b_taps"), sem("b_edge")
        x_mm, x_ev, conv_done, silu_done, xt_mm, xt_ev, chain = (
            sem("b_xmm"), sem("b_xev"), sem("b_conv"), sem("b_silu"), sem("b_xtmm"), sem("b_xtev"), sem("b_chain"))
        dt_mm, dt_act, z_mm, z_act = sem("b_dtmm"), sem("b_dtact"), sem("b_zmm"), sem("b_zact")

        with nc.Block() as block:
            @block.sync
            def _(sp):
                def load_x(b):
                    sp.dma_start(w_x[:, b % RW, :, :], w_in[:, :, COL_XBC + b * P:COL_XBC + (b + 1) * P]).then_inc(s_wx[b % RW], 16)

                def load_z(n):
                    sp.dma_start(w_z[:, n % RZ, :, :], w_in[:, :, z_cols[n]:z_cols[n] + HALF]).then_inc(s_wz[n % RZ], 16)

                load_x(0)
                sp.dma_start(taps_rows[0:CONV_W * XBC_BLOCKS, :], a["conv_w"][0].rearrange("w (b p) -> (w b) p", p=P)).then_inc(s_small, 16)
                sp.dma_start(taps_rows[CONV_W * XBC_BLOCKS:, :], a["conv_b"][0].rearrange("(b p) -> b p", p=P)).then_inc(s_small, 16)
                sp.dma_start(dt_bias[:, 0:SSD_HEADS], a["dt_bias_f"][0].partition_broadcast(P)).then_inc(s_small, 16)
                sp.dma_start(dt_bias[:, SSD_HEADS:], a["dt_bias_b"][0].partition_broadcast(P)).then_inc(s_small, 16)
                sp.dma_start(a_exp[:, 0:SSD_HEADS], a["a_log_f"][0].partition_broadcast(P)).then_inc(s_small, 16)
                sp.dma_start(a_exp[:, SSD_HEADS:], a["a_log_b"][0].partition_broadcast(P)).then_inc(s_small, 16)
                sp.dma_start(w_dt[:, :, :], w_in[:, :, COL_DT:COL_DT + NH2]).then_inc(s_small, 16)
                load_x(1)
                load_x(2)
                load_z(0)
                load_z(1)
                for b in range(RW, XBC_BLOCKS):
                    sp.wait_ge(x_mm, b - RW + 1)
                    load_x(b)
                for n in range(ZB):
                    for t in range(TT):
                        m = n * TT + t
                        sp.wait_ge(z_act, m + 1)
                        sp.dma_start(zg_scr[n // 2, t * P:(t + 1) * P, (n % 2) * HALF:(n % 2 + 1) * HALF],
                                     staged[:, m % RS, :]).then_inc(s_st[m % RS], 16)
                    if n + RZ < ZB:
                        sp.wait_ge(z_mm, (n + 1) * TT)
                        load_z(n + RZ)
                for r in range(RS):
                    sp.wait_ge(s_st[r], 16 * (ZB * TT // RS))

            @block.gpsimd
            def _(pool):
                nc.gpsimd.memset(padded[:, :, 0:2], 0.0).then_inc(edge_done, 1)
                nc.gpsimd.memset(padded[:, :, SEQ + 2:SEQ + 4], 0.0).then_inc(edge_done, 1)

            def gate(act, m, func):
                act.wait_ge(z_mm, m + 1)
                if m >= RS:
                    act.wait_ge(s_st[m % RS], 16 * (m // RS))
                nc.scalar.activation(staged[:, m % RS, :], ps_x[m % 2][:, 0:HALF], func).then_inc(z_act, 1)

            conv_chain = sem("b_convchain")

            @block.scalar
            def _(act):
                act.wait_ge(s_small, 112)
                act.wait_ge(taps_ps, 1)
                nc.scalar.activation(taps[:, :, :], ps_dt[:, 0:(CONV_W + 1) * XBC_BLOCKS].rearrange("p (w b) -> p w b", w=CONV_W + 1),
                                     ACT.Copy).then_inc(taps_done, 1)
                for b in range(XBC_BLOCKS + 2):
                    if b < XBC_BLOCKS:
                        act.wait_ge(x_mm, b + 1)
                        if b >= 2:
                            act.wait_ge(conv_done, b - 1)
                        nc.scalar.activation(padded[:, b % 2, 2:SEQ + 2], ps_x[b % 2][:, :], ACT.Copy).then_inc(x_ev, 1)
                    s = b - 1
                    if 0 <= s < XBC_BLOCKS:
                        act.wait_ge(taps_done, 1)
                        act.wait_ge(conv_done, s + 1)
                        if 2 <= s < 8:
                            act.wait_ge(xt_mm, s - 1)
                        dst = xT[:, s % 2, :] if s < 8 else (BT if s < 12 else CT)[:, s % 4, :]
                        nc.scalar.activation(dst, conv[:, s % 2, :], ACT.Silu, bias=taps[:, CONV_W, s:s + 1]).then_inc(silu_done, 1)
                    r = b - 2
                    if 0 <= r < 8:
                        act.wait_ge(xt_mm, r + 1)
                        nc.scalar.activation(X[:, :, r * P:(r + 1) * P], ps_t[:, :].rearrange("p (t n) -> p t n", t=TT), ACT.Copy).then_inc(xt_ev, 1)
                for m in range(2 * TT):
                    gate(act, m, ACT.Silu)
                for m in range(2 * TT, ZB * TT):
                    gate(act, m, ACT.Sigmoid)
                act.wait_ge(dt_act, 1)
                nc.scalar.activation(neg[:, :, :], neg[:, :, :], ACT.Exp).then_inc(chain, 1)
                nc.scalar.activation(a_exp[:, :], a_exp[:, :], ACT.Exp).then_inc(chain, 1)
                act.wait_ge(chain, 2)
                nc.scalar.activation(neg[:, :, :], neg[:, :, :], ACT.Ln, bias=1.0).then_inc(chain, 1)

            @block.vector
            def _(v):
                links = 0
                v.wait_ge(edge_done, 2)
                v.wait_ge(taps_done, 1)
                for b in range(XBC_BLOCKS):
                    v.wait_ge(x_ev, b + 1)
                    if b >= 2:
                        v.wait_ge(silu_done, b - 1)
                    nc.vector.tensor_scalar(conv[:, b % 2, :], padded[:, b % 2, 0:SEQ], taps[:, 0, b:b + 1], None,
                                            ALU.mult).then_inc(conv_chain, 1)
                    links += 1
                    for w in range(1, CONV_W):
                        v.wait_ge(conv_chain, links)
                        step = nc.vector.scalar_tensor_tensor(out=conv[:, b % 2, :], in0=padded[:, b % 2, w:w + SEQ],
                                                              scalar=taps[:, w, b:b + 1], in1=conv[:, b % 2, :],
                                                              op0=ALU.mult, op1=ALU.add)
                        if w < CONV_W - 1:
                            step.then_inc(conv_chain, 1)
                            links += 1
                    step.then_inc(conv_done, 1)
                v.wait_ge(dt_mm, 1)
                v.wait_ge(s_small, 112)
                nc.vector.tensor_tensor(dt[:, :, :], ps_dt[:, 0:TT * NH2].rearrange("p (t h) -> p t h", t=TT),
                                        dt_bias[:, :].unsqueeze(1).broadcast_to([P, TT, NH2]), ALU.add).then_inc(conv_chain, 1)
                v.wait_ge(conv_chain, links + 1)
                nc.vector.tensor_scalar(neg[:, :, :], dt[:, :, :], -1.0, None, ALU.mult).then_inc(conv_chain, 1)
                v.wait_ge(conv_chain, links + 2)
                nc.vector.tensor_tensor(neg[:, :, :], neg[:, :, :], dt[:, :, :], ALU.min).then_inc(dt_act, 1)
                v.wait_ge(chain, 3)
                nc.vector.scalar_tensor_tensor(out=dt[:, :, :], in0=dt[:, :, :], scalar=0.0, in1=neg[:, :, :],
                                               op0=ALU.max, op1=ALU.add).then_inc(conv_chain, 1)
                v.wait_ge(conv_chain, links + 3)
                nc.vector.scalar_tensor_tensor(out=dA[:, :, :], in0=dt[:, :, :], scalar=-1.0,
                                               in1=a_exp[:, :].unsqueeze(1).broadcast_to([P, TT, NH2]),
                                               op0=ALU.mult, op1=ALU.mult).then_inc(dt_act, 1)

            @block.tensor
            def _(pe):
                pe.wait_ge(s_small, 112)
                nc.tensor.transpose(ps_dt[:, 0:(CONV_W + 1) * XBC_BLOCKS], taps_rows[:, :],
                                    ident[0:(CONV_W + 1) * XBC_BLOCKS, 0:(CONV_W + 1) * XBC_BLOCKS]).then_inc(taps_ps, 1)
                for b in range(XBC_BLOCKS + 2):
                    if b < XBC_BLOCKS:
                        pe.wait_ge(s_wx[b % RW], 16 * (b // RW + 1))
                        if b >= 2:
                            pe.wait_ge(x_ev, b - 1)
                        for h in range(2):
                            for k in range(KD):
                                last = nc.tensor.matmul(ps_x[b % 2][:, h * HALF:(h + 1) * HALF], w_x[:, b % RW, k, :],
                                                        n1T[:, k, h * HALF:(h + 1) * HALF], start=(k == 0), stop=(k == KD - 1))
                        last.then_inc(x_mm, 1)
                    r = b - 2
                    if 0 <= r < 8:
                        pe.wait_ge(silu_done, r + 1)
                        if r:
                            pe.wait_ge(xt_ev, r)
                        for t in range(TT):
                            last = nc.tensor.transpose(ps_t[:, t * P:(t + 1) * P], xT[:, r % 2, t * P:(t + 1) * P], ident[:, :])
                        last.then_inc(xt_mm, 1)
                pe.wait_ge(taps_done, 1)
                for t in range(TT):
                    for k in range(KD):
                        last = nc.tensor.matmul(ps_dt[:, t * NH2:(t + 1) * NH2], n1T[:, k, t * P:(t + 1) * P], w_dt[:, k, :],
                                                start=(k == 0), stop=(k == KD - 1))
                last.then_inc(dt_mm, 1)
                for m in range(ZB * TT):
                    n, t = divmod(m, TT)
                    pe.wait_ge(s_wz[n % RZ], 16 * (n // RZ + 1))
                    if m < 2:
                        pe.wait_ge(x_ev, XBC_BLOCKS)
                    else:
                        pe.wait_ge(z_act, m - 1)
                    for k in range(KD):
                        last = nc.tensor.matmul(ps_x[m % 2][:, 0:HALF], n1T[:, k, t * P:(t + 1) * P], w_z[:, n % RZ, k, :],
                                                start=(k == 0), stop=(k == KD - 1))
                    last.then_inc(z_mm, 1)


def stage_attention(nc, a, opener, banks, sem, w_in, ident, n1T, rpb_scr, na_scr):
    f32 = mybir.dt.float32
    ALU, ACT, AX = mybir.AluOpType, mybir.ActivationFunctionType, mybir.AxisListType
    UPP = 2 * TT
    UNITS = PAIRS * UPP
    SPAN = NA_KH * GRID_W + GRID_W
    first_row = [min(max(2 * j - NA_KH // 2, 0), GRID_H - NA_KH) for j in range(TT)]
    inner = [0 < 2 * j + 1 - NA_KH // 2 <= GRID_H - NA_KH and 2 * j - NA_KH // 2 >= 0 for j in range(TT)]
    width = [SPAN if inner[j] else SPAN - GRID_W for j in range(TT)]
    slot0 = [first_row[j] - 2 * j + NA_KH - 1 for j in range(TT)]
    GROUPS6 = 6
    ctx = ExitStack()
    with ctx:
        sb = opener(ctx)
        w = sb("w_qkv", [P, 2, KD, 3, P])
        qT = sb("qT", [P, 2, SEQ])
        kT = sb("kT", [P, 2, SEQ])
        vT = sb("vT", [P, SEQ])
        V = sb("V", [P, 2, TT, P])
        bias = sb("bias", [P, 2, SLOTS, GRID_W])
        colmask = sb("colmask", [P, GRID_W])
        S = sb("S", [P, 2, SPAN])
        Pr = sb("Pr", [P, 2, SPAN])
        PT = sb("PT", [P, 2, 5, P])
        nmax = sb("nmax", [P, 2])
        rsum = sb("rsum", [P, 2])
        rinv = sb("rinv", [P, 2])
        O = sb("O", [P, 2, TT, P])
        ps_s = [banks(ctx, f"ps_s{i}", 2) for i in range(2)]
        ps_p = banks(ctx, "ps_p", 2)
        ps_o = banks(ctx, "ps_o", 1)
        ps_j = banks(ctx, "ps_j", 1)

        s_w = [sem("c_w0"), sem("c_w1")]
        s_bias = [sem("c_bias0"), sem("c_bias1")]
        s_out = [sem("c_out0"), sem("c_out1")]
        mask_zero, mask_done, bias_done = sem("c_mz"), sem("c_md"), sem("c_bd")
        qk_done, max_done, exp_done, pt_mm, pt_ev, pv_done, o_done = (
            sem("c_qk"), sem("c_max"), sem("c_exp"), sem("c_ptmm"), sem("c_ptev"), sem("c_pv"), sem("c_o"))
        pt_ev2, rinv_done = sem("c_ptev2"), sem("c_rinv")
        proj_mm, proj_ev, chain = sem("c_projmm"), sem("c_projev"), sem("c_chain")

        def groups_before(p):
            return p * (GROUPS6 + 2)

        with nc.Block() as block:
            @block.sync
            def _(sp):
                def load_w(p):
                    for part in range(3):
                        sp.dma_start(w[:, p % 2, :, part, :],
                                     w_in[:, :, COL_QKV + part * DM + p * P:COL_QKV + part * DM + (p + 1) * P]).then_inc(s_w[p % 2], 16)

                def load_bias(h):
                    for r in range(2):
                        src = rpb_scr[h, 1 - r:1 - r + SLOTS, :, :].rearrange("s q k -> q s k")
                        sp.dma_start(bias[r * GRID_W:(r + 1) * GRID_W, h % 2, :, :], src).then_inc(s_bias[h % 2], 16)

                load_w(0)
                load_bias(0)
                load_w(1)
                load_bias(1)
                for p in range(PAIRS):
                    for hh in range(2):
                        if 2 * p + hh + 2 < NA_HEADS:
                            sp.wait_ge(max_done, (2 * p + hh + 1) * TT)
                            load_bias(2 * p + hh + 2)
                    if p + 2 < PAIRS:
                        sp.wait_ge(proj_mm, groups_before(p + 1))
                        load_w(p + 2)
                    sp.wait_ge(o_done, (p + 1) * UPP)
                    sp.dma_start(na_scr[:, p * P:(p + 1) * P].rearrange("(t q) n -> q t n", q=P), O[:, p % 2, :, :]).then_inc(s_out[p % 2], 16)
                for i in range(2):
                    sp.wait_ge(s_out[i], 16 * (PAIRS // 2))

            @block.gpsimd
            def _(pool):
                nc.gpsimd.memset(colmask[:, :], 0.0).then_inc(mask_zero, 1)
                pool.wait_ge(mask_zero, 1)
                edge = GRID_W - NA_KW
                for r in range(2):
                    m = colmask[r * GRID_W:(r + 1) * GRID_W, :]
                    nc.gpsimd.affine_select(out=m[:, 0:edge], in_=m[:, 0:edge], compare_op=ALU.is_ge, fill=MASKED,
                                            base=NA_KW // 2, pattern=[[1, edge]], channel_multiplier=-1).then_inc(mask_zero, 1)
                    pool.wait_ge(mask_zero, 2 + r)
                    nc.gpsimd.affine_select(out=m[:, NA_KW:], in_=m[:, NA_KW:], compare_op=ALU.is_ge, fill=MASKED,
                                            base=NA_KW // 2 - 1 - NA_KW, pattern=[[-1, edge]], channel_multiplier=1).then_inc(mask_done, 1)
                pool.wait_ge(mask_done, 2)
                for h in range(NA_HEADS):
                    pool.wait_ge(s_bias[h % 2], 32 * (h // 2 + 1))
                    nc.gpsimd.tensor_tensor(bias[:, h % 2, :, :], bias[:, h % 2, :, :],
                                            colmask[:, :].unsqueeze(1).broadcast_to([P, SLOTS, GRID_W]), ALU.add).then_inc(bias_done, 1)

            def proj_group(p, g):
                return groups_before(p) + g + 1

            @block.scalar
            def _(act):
                def proj_evac(p, g):
                    act.wait_ge(proj_mm, proj_group(p, g))
                    if g < 6:
                        dst = (qT[:, p % 2, :], kT[:, p % 2, :], vT[:, :])[g // 2]
                        nc.scalar.activation(dst[:, (g % 2) * HALF:(g % 2 + 1) * HALF], ps_j[:, :], ACT.Copy).then_inc(proj_ev, 1)
                    else:
                        q = g - 6
                        nc.scalar.activation(V[:, p % 2, 4 * q:4 * q + 4, :], ps_j[:, :].rearrange("p (t n) -> p t n", t=4),
                                             ACT.Copy).then_inc(proj_ev, 1)

                def probs_evac(u):
                    j = u % TT
                    act.wait_ge(pt_mm, u + 1)
                    if u >= 2:
                        act.wait_ge(pv_done, u - 1)
                    nc.scalar.activation(PT[:, u % 2, 0:4, :], ps_p[:, 0:HALF].rearrange("p (b n) -> p b n", b=4), ACT.Copy).then_inc(pt_ev, 1)
                    if inner[j]:
                        nc.scalar.activation(PT[0:GRID_W, u % 2, 4, :], ps_p[0:GRID_W, HALF:HALF + P], ACT.Copy).then_inc(pt_ev2, 1)

                for g in range(8):
                    proj_evac(0, g)
                for u in range(UNITS + 1):
                    if u >= 1:
                        probs_evac(u - 1)
                    if u < UNITS:
                        act.wait_ge(max_done, u + 1)
                        if u >= 2:
                            act.wait_ge(pt_mm, u - 1)
                        n = width[u % TT]
                        nc.scalar.activation(Pr[:, u % 2, 0:n], S[:, u % 2, 0:n], ACT.Exp, bias=nmax[:, u % 2:u % 2 + 1],
                                             accum_out=rsum[:, u % 2:u % 2 + 1]).then_inc(exp_done, 1)
                        p, s = divmod(u, UPP)
                        if s % 2 == 1 and p + 1 < PAIRS:
                            proj_evac(p + 1, s // 2)

            inner_before = lambda u: (u // TT) * sum(inner) + sum(inner[:u % TT])

            @block.vector
            def _(v):
                links = 0

                def scale_out(u):
                    p, s = divmod(u, UPP)
                    hh, j = divmod(s, TT)
                    v.wait_ge(exp_done, u + 1)
                    nc.vector.reciprocal(rinv[:, u % 2:u % 2 + 1], rsum[:, u % 2:u % 2 + 1]).then_inc(rinv_done, 1)
                    v.wait_ge(pv_done, u + 1)
                    v.wait_ge(rinv_done, u + 1)
                    if s == 0 and p >= 2:
                        v.wait_ge(s_out[p % 2], 16 * (p // 2))
                    nc.vector.tensor_scalar(O[:, p % 2, j, hh * HEADDIM:(hh + 1) * HEADDIM], ps_o[:, 0:HEADDIM],
                                            rinv[:, u % 2:u % 2 + 1], None, ALU.mult).then_inc(o_done, 1)

                for u in range(UNITS + 1):
                    if u < UNITS:
                        h, j = divmod(u, TT)
                        n = width[j]
                        if j == 0:
                            v.wait_ge(bias_done, h + 1)
                        v.wait_ge(qk_done, u + 1)
                        if u >= 2:
                            v.wait_ge(exp_done, u - 1)
                        nc.vector.scalar_tensor_tensor(
                            out=S[:, u % 2, 0:n], in0=ps_s[u % 2][:, 0:n], scalar=HEADDIM ** -0.5,
                            in1=bias[:, h % 2, slot0[j]:slot0[j] + n // GRID_W, :].rearrange("p s c -> p (s c)"),
                            op0=ALU.mult, op1=ALU.add).then_inc(chain, 1)
                        links += 1
                        v.wait_ge(chain, links)
                        if inner[j]:
                            nc.vector.memset(S[0:GRID_W, u % 2, n - GRID_W:n], MASKED)
                            nc.vector.memset(S[GRID_W:P, u % 2, 0:GRID_W], MASKED).then_inc(chain, 1)
                            links += 1
                            v.wait_ge(chain, links)
                        nc.vector.tensor_reduce(nmax[:, u % 2:u % 2 + 1], S[:, u % 2, 0:n], AX.X, ALU.max, negate=True).then_inc(max_done, 1)
                    if u >= 1:
                        scale_out(u - 1)

            @block.tensor
            def _(pe):
                def proj_steps(p, g, lo, hi):
                    end = 8 if g < 6 else 4
                    if lo == 0:
                        if g == 0 :
                            pe.wait_ge(s_w[p % 2], 48 * (p // 2 + 1))
                        if groups_before(p) + g:
                            pe.wait_ge(proj_ev, groups_before(p) + g)
                    for k in range(lo, hi):
                        if g < 6:
                            half = g % 2
                            last = nc.tensor.matmul(ps_j[:, :], w[:, p % 2, k, g // 2, :], n1T[:, k, half * HALF:(half + 1) * HALF],
                                                    start=(k == 0), stop=(k == KD - 1))
                        else:
                            t = 4 * (g - 6) + k
                            last = nc.tensor.transpose(ps_j[:, k * P:(k + 1) * P], vT[:, t * P:(t + 1) * P], ident[:, :])
                    if hi == end:
                        last.then_inc(proj_mm, 1)

                for g in range(8):
                    proj_steps(0, g, 0, 8 if g < 6 else 4)
                for u in range(UNITS + 1):
                    if u < UNITS:
                        p, s = divmod(u, UPP)
                        hh, j = divmod(s, TT)
                        if s == 0:
                            pe.wait_ge(proj_ev, groups_before(p + 1))
                        if u >= 2:
                            pe.wait_ge(max_done, u - 1)
                        rows = slice(hh * HEADDIM, (hh + 1) * HEADDIM)
                        k0 = first_row[j] * GRID_W
                        last = nc.tensor.matmul(ps_s[u % 2][:, 0:HALF], qT[rows, p % 2, j * P:(j + 1) * P],
                                                kT[rows, p % 2, k0:k0 + HALF], start=True, stop=True)
                        if inner[j]:
                            last = nc.tensor.matmul(ps_s[u % 2][:, HALF:HALF + GRID_W], qT[rows, p % 2, j * P:(j + 1) * P],
                                                    kT[rows, p % 2, k0 + HALF:k0 + HALF + GRID_W], start=True, stop=True)
                        last.then_inc(qk_done, 1)
                    if u >= 1:
                        t = u - 1
                        j = t % TT
                        pe.wait_ge(exp_done, t + 1)
                        if t >= 1:
                            pe.wait_ge(pt_ev, t)
                            pe.wait_ge(pt_ev2, inner_before(t)) if inner_before(t) else None
                        for b in range(4):
                            last = nc.tensor.transpose(ps_p[:, b * P:(b + 1) * P], Pr[:, t % 2, b * P:(b + 1) * P], ident[:, :])
                        if inner[j]:
                            last = nc.tensor.transpose(ps_p[0:GRID_W, HALF:HALF + P], Pr[:, t % 2, HALF:HALF + GRID_W], ident[:, :])
                        last.then_inc(pt_mm, 1)
                    if u < UNITS:
                        p, s = divmod(u, UPP)
                        if p + 1 < PAIRS:
                            g, odd = divmod(s, 2)
                            n = 4 if g < 6 else 2
                            proj_steps(p + 1, g, odd * n, odd * n + n)
                    if u >= 1:
                        t = u - 1
                        p, s = divmod(t, UPP)
                        hh, j = divmod(s, TT)
                        pe.wait_ge(pt_ev, t + 1)
                        if inner[j]:
                            pe.wait_ge(pt_ev2, inner_before(t) + 1)
                        if t >= 1:
                            pe.wait_ge(o_done, t)
                        b0 = first_row[j] // 2
                        for b in range(5 if inner[j] else 4):
                            keys = P if b < 4 else GRID_W
                            last = nc.tensor.matmul(ps_o[:, 0:HEADDIM], PT[0:keys, t % 2, b, :],
                                                    V[0:keys, p % 2, b0 + b, hh * HEADDIM:(hh + 1) * HEADDIM],
                                                    start=(b == 0), stop=(b == (4 if inner[j] else 3)))
                        last.then_inc(pv_done, 1)


def stage_ssd(nc, a, opener, banks, sem, consts, X, BT, CT, dt, dA, zg_scr, y_rstd):
    f32 = mybir.dt.float32
    ALU, ACT, AX = mybir.AluOpType, mybir.ActivationFunctionType, mybir.AxisListType
    ident, upto, since, after, before, ones = consts
    H, GP = SSD_HEADS, HPG * HEADDIM
    UNITS = TT * GROUPS
    TAB = TT * H
    ctx = ExitStack()
    with ctx:
        sb = opener(ctx)
        tabs = sb("tabs", [P, 6, TT, H])
        w_state = sb("w_state", [P, 2, TT, H])
        Bt = sb("Bt", [P, TT, GROUPS * STATE])
        back = sb("back", [P, TT, DM])
        fwd = sb("fwd", [P, 2, DM])
        d_skip = sb("d_skip", [P, H])
        xb_state = sb("xb_state", [P, 2, DM])
        tmp = sb("tmpD", [P, DM])
        x_dt = sb("x_dt", [P, 2, 2, DM])
        xf_state = sb("xf_state", [P, DM])
        rhs = sb("rhsD", [P, 2, 2, HPG, P])
        E = sb("E", [P, 2, HPG, P])
        cb = sb("cb", [P, 2, P])
        M = sb("M", [P, 2, 2, HPG, P])
        off = sb("off", [P, 2, GP])
        skip = sb("skip", [P, GP])
        Y = sb("Y", [P, DM])
        z = sb("z", [P, 2, DM])
        sumsq = sb("sumsqD", [P, TT])
        ps_a = [banks(ctx, f"ps_a{i}", 1) for i in range(2)]
        ps_cb = banks(ctx, "ps_cb", 1)
        ps_y = [banks(ctx, f"ps_y{i}", 1) for i in range(2)]
        ps_off = banks(ctx, "ps_off", 1)
        ps_st = banks(ctx, "ps_st", 2)

        s_skip, tab_mm, tab_exp, w_done = sem("d_skip"), sem("d_tabmm"), sem("d_tabexp"), sem("d_w")
        s_z = [sem("d_z0"), sem("d_z1")]
        bt_mm, bt_ev = sem("d_btmm"), sem("d_btev")
        xb_done, bst_mm, bst_done, zero_done = sem("d_xb"), sem("d_bstmm"), sem("d_bst"), sem("d_zero")
        rhs_done, a_mm, e_done, cb_mm, m_done, y_mm, y_done = (
            sem("d_rhs"), sem("d_amm"), sem("d_e"), sem("d_cbmm"), sem("d_m"), sem("d_ymm"), sem("d_y"))
        cb_read, off_mm, off_read, xdt_done, xf_done, fst_mm, fwd_done, chain, gated, bchain = (
            sem("d_cbread"), sem("d_offmm"), sem("d_offread"), sem("d_xdt"), sem("d_xf"), sem("d_fstmm"),
            sem("d_fwd"), sem("d_chain"), sem("d_gated"), sem("d_bchain"))
        sq_done, rs_done = sem("d_sq"), sem("d_rs")

        def by_head(t, n=H, w=HEADDIM):
            return t.unsqueeze(2).broadcast_to([P, n, w])

        def heads(t):
            return t.rearrange("p (h e) -> p h e", e=HEADDIM)

        with nc.Block() as block:
            @block.sync
            def _(sp):
                sp.dma_start(d_skip[:, :], a["d_skip"][0].partition_broadcast(P)).then_inc(s_skip, 16)
                for c in range(TT):
                    if c >= 2:
                        sp.wait_ge(gated, c - 1)
                    sp.dma_start(z[:, c % 2, :], zg_scr[0, c * P:(c + 1) * P, :]).then_inc(s_z[c % 2], 16)

            @block.gpsimd
            def _(pool):
                nc.gpsimd.memset(back[:, TT - 1, :], 0.0).then_inc(zero_done, 1)
                nc.gpsimd.memset(fwd[:, 0, :], 0.0).then_inc(zero_done, 1)

                def build_rhs(u):
                    c, g = divmod(u, GROUPS)
                    if u >= 2:
                        pool.wait_ge(a_mm, u - 1)
                    for d, mask in ((0, upto), (1, since)):
                        nc.gpsimd.tensor_tensor(rhs[:, u % 2, d, :, :], mask[:, :].unsqueeze(1).broadcast_to([P, HPG, P]),
                                                dA[:, c, d * H + g * HPG:d * H + (g + 1) * HPG].unsqueeze(2).broadcast_to([P, HPG, P]),
                                                ALU.mult).then_inc(rhs_done, 1)

                def scale_x(c):
                    if c >= 2:
                        pool.wait_ge(y_mm, (c - 1) * GROUPS)
                    for d in range(2):
                        nc.gpsimd.tensor_tensor(heads(x_dt[:, c % 2, d, :]), heads(X[:, c, :]), by_head(dt[:, c, d * H:(d + 1) * H]),
                                                ALU.mult).then_inc(xdt_done, 1)

                def scale_for_state(c):
                    if c < TT - 1:
                        pool.wait_ge(w_done, 2)
                        if c >= 1:
                            pool.wait_ge(fst_mm, c)
                        nc.gpsimd.tensor_tensor(heads(xf_state[:, :]), heads(X[:, c, :]), by_head(w_state[:, 0, c, :]),
                                                ALU.mult).then_inc(xf_done, 1)

                scale_x(0)
                build_rhs(0)
                build_rhs(1)
                scale_for_state(0)
                for u in range(UNITS):
                    if u % GROUPS == 1 and u // GROUPS + 1 < TT:
                        scale_x(u // GROUPS + 1)
                    if u + 2 < UNITS:
                        build_rhs(u + 2)
                    if u % GROUPS == GROUPS - 1:
                        scale_for_state(u // GROUPS + 1)

            @block.scalar
            def _(act):
                act.wait_ge(tab_mm, 1)
                nc.scalar.activation(tabs[:, 0:4, :, :].rearrange("p k c h -> p (k c h)"), ps_a[0][:, :], ACT.Exp).then_inc(tab_exp, 1)
                nc.scalar.activation(tabs[:, 4:6, :, :].rearrange("p k c h -> p (k c h)"), ps_a[1][:, 0:2 * TAB], ACT.Exp).then_inc(tab_exp, 1)
                for c in range(TT):
                    act.wait_ge(bt_mm, c + 1)
                    nc.scalar.activation(Bt[:, c, :], ps_y[c % 2][:, :], ACT.Copy).then_inc(bt_ev, 1)
                for u in range(UNITS):
                    act.wait_ge(a_mm, u + 1)
                    if u >= 2:
                        act.wait_ge(m_done, 2 * (u - 1))
                    nc.scalar.activation(E[:, u % 2, :, :].rearrange("p h l -> p (h l)"), ps_a[u % 2][:, :], ACT.Exp).then_inc(e_done, 1)
                act.wait_ge(rs_done, 1)
                nc.scalar.activation(y_rstd[:, :], y_rstd[:, :], ACT.Sqrt).then_inc(sq_done, 1)

            @block.vector
            def _(v):
                v.wait_ge(tab_exp, 2)
                for d in range(2):
                    nc.vector.tensor_tensor(w_state[:, d, :, :], tabs[:, 2 + d, :, :], dt[:, :, d * H:(d + 1) * H], ALU.mult).then_inc(w_done, 1)
                v.wait_ge(w_done, 2)

                def scale_xb(n):
                    c = TT - 1 - n
                    if n >= 2:
                        v.wait_ge(bst_mm, n - 1)
                    nc.vector.tensor_tensor(heads(xb_state[:, n % 2, :]), heads(X[:, c, :]), by_head(w_state[:, 1, c, :]), ALU.mult).then_inc(xb_done, 1)

                scale_xb(0)
                v.wait_ge(zero_done, 2)
                for n in range(TT - 1):
                    c = TT - 1 - n
                    if n + 1 < TT - 1:
                        scale_xb(n + 1)
                    if n:
                        v.wait_ge(bst_done, n)
                    nc.vector.tensor_tensor(heads(tmp[:, :]), heads(back[:, c, :]), by_head(tabs[:, 5, c, :]), ALU.mult).then_inc(bchain, 1)
                    v.wait_ge(bchain, n + 1)
                    v.wait_ge(bst_mm, n + 1)
                    nc.vector.tensor_tensor(back[:, c - 1, :], tmp[:, :], ps_st[:, :], ALU.add).then_inc(bst_done, 1)
                v.wait_ge(bst_done, TT - 1)
                v.wait_ge(s_skip, 16)

                links = 0
                for u in range(UNITS + 1):
                    if u < UNITS:
                        c, g = divmod(u, GROUPS)
                        v.wait_ge(cb_mm, u + 1)
                        if u >= 1:
                            v.wait_ge(m_done, 2 * u)
                        for d, mask in ((0, upto), (1, since)):
                            nc.vector.tensor_tensor(cb[:, d, :], ps_cb[:, 0:P], mask[:, :], ALU.mult).then_inc(cb_read, 1)
                        v.wait_ge(cb_read, 2 * u + 2)
                        v.wait_ge(e_done, u + 1)
                        if u >= 2:
                            v.wait_ge(y_mm, u - 1)
                        for d in range(2):
                            nc.vector.tensor_tensor(M[:, u % 2, d, :, :], E[:, u % 2, :, :],
                                                    cb[:, d, :].unsqueeze(1).broadcast_to([P, HPG, P]), ALU.mult).then_inc(m_done, 1)
                    if u >= 1:
                        w = u - 1
                        c, g = divmod(w, GROUPS)
                        cols = slice(g * GP, (g + 1) * GP)
                        v.wait_ge(off_mm, w + 1)
                        if w:
                            v.wait_ge(y_done, w)
                        for d in range(2):
                            nc.vector.tensor_tensor(heads(off[:, d, :]), heads(ps_off[:, d * GP:(d + 1) * GP]),
                                                    by_head(tabs[:, d, c, g * HPG:(g + 1) * HPG], HPG), ALU.mult).then_inc(off_read, 1)
                        nc.vector.tensor_tensor(heads(skip[:, :]), heads(X[:, c, cols]), by_head(d_skip[:, g * HPG:(g + 1) * HPG], HPG),
                                                ALU.mult).then_inc(chain, 1)
                        v.wait_ge(off_read, 2 * w + 2)
                        nc.vector.tensor_tensor(off[:, 0, :], off[:, 0, :], off[:, 1, :], ALU.add).then_inc(chain, 1)
                        v.wait_ge(chain, links + 2)
                        nc.vector.tensor_tensor(off[:, 0, :], off[:, 0, :], skip[:, :], ALU.add).then_inc(chain, 1)
                        links += 3
                        v.wait_ge(chain, links)
                        v.wait_ge(y_mm, w + 1)
                        if g == 0 and c:
                            v.wait_ge(gated, c)
                        nc.vector.tensor_tensor(Y[:, cols], off[:, 0, :], ps_y[w % 2][:, 0:GP], ALU.add).then_inc(y_done, 1)
                        if g == GROUPS - 1:
                            if c < TT - 1:
                                if c:
                                    v.wait_ge(fwd_done, c)
                                nc.vector.tensor_tensor(heads(tmp[:, :]), heads(fwd[:, c % 2, :]), by_head(tabs[:, 4, c, :]), ALU.mult).then_inc(chain, 1)
                                links += 1
                                v.wait_ge(chain, links)
                                v.wait_ge(fst_mm, c + 1)
                                nc.vector.tensor_tensor(fwd[:, (c + 1) % 2, :], tmp[:, :], ps_st[:, :], ALU.add).then_inc(fwd_done, 1)
                            v.wait_ge(s_z[c % 2], 16 * (c // 2 + 1))
                            v.wait_ge(y_done, w + 1)
                            v.wait_ge(xdt_done, 2 * (c + 1))
                            v.wait_ge(xf_done, min(c + 1, TT - 1))
                            if c == TT - 1:
                                v.wait_ge(chain, links)
                            nc.vector.tensor_tensor(X[:, c, :], Y[:, :], z[:, c % 2, :], ALU.mult).then_inc(gated, 1)
                            v.wait_ge(gated, c + 1)
                            nc.vector.tensor_tensor_reduce(out=tmp[:, :], in0=X[:, c, :], in1=X[:, c, :], scale=1.0, scalar=0.0,
                                                           op0=ALU.mult, op1=ALU.add, accum_out=sumsq[:, c:c + 1]).then_inc(chain, 1)
                            links += 1
                            v.wait_ge(chain, links)
                nc.vector.tensor_scalar(y_rstd[:, :], sumsq[:, :], 1.0 / DM, EPS, ALU.mult, ALU.add).then_inc(rs_done, 1)
                v.wait_ge(sq_done, 1)
                nc.vector.reciprocal(y_rstd[:, :], y_rstd[:, :]).then_inc(rs_done, 1)

            @block.tensor
            def _(pe):
                for i, (mat, d) in enumerate(((upto, 0), (since, 1), (after, 0), (before, 1))):
                    nc.tensor.matmul(ps_a[0][:, i * TAB:(i + 1) * TAB], mat[:, :], dA[:, :, d * H:(d + 1) * H], start=True, stop=True)
                for d in range(2):
                    last = nc.tensor.matmul(ps_a[1][:, d * TAB:(d + 1) * TAB], ones[:, :], dA[:, :, d * H:(d + 1) * H], start=True, stop=True)
                last.then_inc(tab_mm, 1)
                for c in range(TT):
                    if c >= 2:
                        pe.wait_ge(bt_ev, c - 1)
                    for g in range(GROUPS):
                        last = nc.tensor.transpose(ps_y[c % 2][:, g * STATE:(g + 1) * STATE], BT[:, g, c * P:(c + 1) * P], ident[:, :])
                    last.then_inc(bt_mm, 1)

                def states(c, x_src, done):
                    for g in range(GROUPS):
                        last = nc.tensor.matmul(ps_st[:, g * GP:(g + 1) * GP], Bt[:, c, g * STATE:(g + 1) * STATE],
                                                x_src[:, g * GP:(g + 1) * GP], start=True, stop=True)
                    last.then_inc(done, 1)

                pe.wait_ge(bt_ev, TT)
                for n in range(TT - 1):
                    pe.wait_ge(xb_done, n + 1)
                    if n:
                        pe.wait_ge(bst_done, n)
                    states(TT - 1 - n, xb_state[:, n % 2, :], bst_mm)
                pe.wait_ge(tab_exp, 2)

                def decays(u):
                    pe.wait_ge(rhs_done, 2 * u + 2)
                    if u >= 2:
                        pe.wait_ge(e_done, u - 1)
                    nc.tensor.matmul(ps_a[u % 2][:, :], after[:, :], rhs[:, u % 2, 0, :, :].rearrange("p h l -> p (h l)"), start=True, stop=False)
                    nc.tensor.matmul(ps_a[u % 2][:, :], before[:, :], rhs[:, u % 2, 1, :, :].rearrange("p h l -> p (h l)"),
                                     start=False, stop=True).then_inc(a_mm, 1)

                def scores(u):
                    c, g = divmod(u, GROUPS)
                    if u:
                        pe.wait_ge(cb_read, 2 * u)
                    nc.tensor.matmul(ps_cb[:, 0:P], BT[:, g, c * P:(c + 1) * P], CT[:, g, c * P:(c + 1) * P],
                                     start=True, stop=True).then_inc(cb_mm, 1)

                decays(0)
                scores(0)
                pe.wait_ge(bst_done, TT - 1)
                for u in range(UNITS):
                    c, g = divmod(u, GROUPS)
                    if u + 1 < UNITS:
                        decays(u + 1)
                        scores(u + 1)
                    if g == 0:
                        pe.wait_ge(fwd_done, c) if c else pe.wait_ge(zero_done, 2)
                    if u:
                        pe.wait_ge(off_read, 2 * u)
                    cols = slice(g * GP, (g + 1) * GP)
                    for d, state in ((0, fwd[:, c % 2, cols]), (1, back[:, c, cols])):
                        last = nc.tensor.matmul(ps_off[:, d * GP:(d + 1) * GP], CT[:, g, c * P:(c + 1) * P], state, start=True, stop=True)
                    last.then_inc(off_mm, 1)
                    pe.wait_ge(m_done, 2 * u + 2)
                    pe.wait_ge(xdt_done, 2 * (c + 1))
                    if u >= 2:
                        pe.wait_ge(y_done, u - 1)
                    for h in range(HPG):
                        hc = slice(g * GP + h * HEADDIM, g * GP + (h + 1) * HEADDIM)
                        for d in range(2):
                            last = nc.tensor.matmul(ps_y[u % 2][:, h * HEADDIM:(h + 1) * HEADDIM], M[:, u % 2, d, h, :],
                                                    x_dt[:, c % 2, d, hc], start=(d == 0), stop=(d == 1))
                    last.then_inc(y_mm, 1)
                    if g == GROUPS - 2 and c < TT - 1:
                        pe.wait_ge(xf_done, c + 1)
                        if c:
                            pe.wait_ge(fwd_done, c)
                        states(c, xf_state, fst_mm)


def stage_merge(nc, a, opener, banks, sem, ident, X, y_rstd, zg_scr, na_scr, mix_scr):
    ALU, ACT = mybir.AluOpType, mybir.ActivationFunctionType
    ctx = ExitStack()
    with ctx:
        sb = opener(ctx)
        w_br = sb("w_br", [P, 2, KD, DM])
        g_rows = sb("g_rows", [KD, P])
        g_cols = sb("g_cols", [P, KD])
        o_in = sb("o_in", [P, 2, DM])
        gates = sb("gates", [P, 2, 2, DM])
        yT = sb("yT", [P, 2, KD, P])
        oT = sb("oT", [P, 2, KD, P])
        mixed = sb("mixed", [P, 2, DM])
        side = sb("side", [P, DM])
        ps_t = [banks(ctx, f"ps_tE{i}", 2) for i in range(2)]
        ps_b = [banks(ctx, f"ps_bE{i}", 2) for i in range(2)]
        s_w = [[sem(f"e_w{i}{h}") for h in range(2)] for i in range(2)]
        s_g = sem("e_g")
        s_in = [sem("e_in0"), sem("e_in1")]
        s_out = [sem("e_out0"), sem("e_out1")]
        g_mm, g_ev, t_mm, t_ev, b_mm, m_done, chain = (
            sem("e_gmm"), sem("e_gev"), sem("e_tmm"), sem("e_tev"), sem("e_bmm"), sem("e_m"), sem("e_chain"))

        with nc.Block() as block:
            @block.sync
            def _(sp):
                def load(t):
                    rows = slice(t * P, (t + 1) * P)
                    sp.dma_start(o_in[:, t % 2, :], na_scr[rows, :]).then_inc(s_in[t % 2], 16)
                    for i in range(2):
                        sp.dma_start(gates[:, t % 2, i, :], zg_scr[1 + i, rows, :]).then_inc(s_in[t % 2], 16)

                sp.dma_start(g_rows[:, :], a["ssd_norm_g"][0].rearrange("(k p) -> k p", p=P)).then_inc(s_g, 16)
                for i, name in enumerate(("w_ssd_br", "w_na_br")):
                    for h in range(2):
                        cols = slice(h * HALF, (h + 1) * HALF)
                        sp.dma_start(w_br[:, i, :, cols], a[name][0].rearrange("(k p) n -> p k n", p=P)[:, :, cols]).then_inc(s_w[i][h], 16)
                    if i == 0:
                        load(0)
                load(1)
                for t in range(TT):
                    sp.wait_ge(m_done, t + 1)
                    sp.dma_start(mix_scr[t * P:(t + 1) * P, :], mixed[:, t % 2, :]).then_inc(s_out[t % 2], 16)
                    if t + 2 < TT:
                        sp.wait_ge(t_mm, 2 * (t + 1))
                        load(t + 2)
                for i in range(2):
                    sp.wait_ge(s_out[i], 16 * (TT // 2))

            @block.scalar
            def _(act):
                act.wait_ge(g_mm, 1)
                nc.scalar.activation(g_cols[:, :], ps_b[0][:, 0:KD], ACT.Copy).then_inc(g_ev, 1)
                act.wait_ge(g_ev, 1)
                for t in range(TT):
                    act.wait_ge(t_mm, 2 * t + 1)
                    if t >= 2:
                        act.wait_ge(b_mm, 2 * (t - 2) + 1)
                    for k in range(KD):
                        last = nc.scalar.activation(yT[:, t % 2, k, :], ps_t[0][:, k * P:(k + 1) * P], ACT.Copy, scale=g_cols[:, k:k + 1])
                    last.then_inc(t_ev, 1)
                    act.wait_ge(t_mm, 2 * t + 2)
                    if t >= 2:
                        act.wait_ge(b_mm, 2 * (t - 2) + 2)
                    nc.scalar.activation(oT[:, t % 2, :, :], ps_t[1][:, :].rearrange("p (k n) -> p k n", k=KD), ACT.Copy).then_inc(t_ev, 1)

            @block.vector
            def _(v):
                links = 0
                for t in range(TT):
                    v.wait_ge(s_in[t % 2], 48 * (t // 2 + 1))
                    v.wait_ge(b_mm, 2 * t + 1)
                    if t >= 2:
                        v.wait_ge(s_out[t % 2], 16 * (t // 2))
                    nc.vector.scalar_tensor_tensor(out=mixed[:, t % 2, :], in0=ps_b[0][:, :], scalar=y_rstd[:, t:t + 1],
                                                   in1=gates[:, t % 2, 0, :], op0=ALU.mult, op1=ALU.mult).then_inc(chain, 1)
                    v.wait_ge(b_mm, 2 * t + 2)
                    if t:
                        v.wait_ge(m_done, t)
                    nc.vector.tensor_tensor(side[:, :], ps_b[1][:, :], gates[:, t % 2, 1, :], ALU.mult).then_inc(chain, 1)
                    links += 2
                    v.wait_ge(chain, links)
                    nc.vector.tensor_tensor(mixed[:, t % 2, :], mixed[:, t % 2, :], side[:, :], ALU.add).then_inc(m_done, 1)

            @block.tensor
            def _(pe):
                pe.wait_ge(s_g, 16)
                nc.tensor.transpose(ps_b[0][:, 0:KD], g_rows[:, :], ident[0:KD, 0:KD]).then_inc(g_mm, 1)

                def turn(t):
                    pe.wait_ge(s_in[t % 2], 48 * (t // 2 + 1))
                    for i, src in ((0, X[:, t, :]), (1, o_in[:, t % 2, :])):
                        if t:
                            pe.wait_ge(t_ev, 2 * (t - 1) + i + 1)
                        for k in range(KD):
                            last = nc.tensor.transpose(ps_t[i][:, k * P:(k + 1) * P], src[:, k * P:(k + 1) * P], ident[:, :])
                        last.then_inc(t_mm, 1)

                turn(0)
                pe.wait_ge(g_ev, 1)
                for t in range(TT):
                    if t + 1 < TT:
                        turn(t + 1)
                    for i, lhs in ((0, yT), (1, oT)):
                        pe.wait_ge(t_ev, 2 * t + i + 1)
                        if t:
                            pe.wait_ge(chain, 2 * (t - 1) + i + 1)
                        for h in range(2):
                            pe.wait_ge(s_w[i][h], 16)
                            for k in range(KD):
                                last = nc.tensor.matmul(ps_b[i][:, h * HALF:(h + 1) * HALF], lhs[:, t % 2, k, :],
                                                        w_br[:, i, k, h * HALF:(h + 1) * HALF], start=(k == 0), stop=(k == KD - 1))
                        last.then_inc(b_mm, 1)


def stage_peer(nc, a, opener, banks, sem, ident, mod_scr, mix_scr, out, s_out):
    f32, u32 = mybir.dt.float32, mybir.dt.uint32
    ALU, ACT, AX = mybir.AluOpType, mybir.ActivationFunctionType, mybir.AxisListType
    RU, RV, RD, RH, RI = 4, 4, 4, 3, 3
    ctx = ExitStack()
    with ctx:
        sb = opener(ctx)
        w_out = sb("w_out", [P, KD, DM])
        w_q = sb("w_q", [P, KD, QW])
        keys = sb("keys", [P, 2, P])
        keysT = sb("keysT", [P, 2, P])
        gate1 = sb("gate1", [P, DM])
        shift2 = sb("shift2", [P, DM])
        gain2 = sb("gain2", [P, DM])
        gate2 = sb("gate2", [P, DM])
        final_g = sb("final_g", [P, DM])
        h = sb("h", [P, RH, DM])
        n2 = sb("n2", [P, 2, DM])
        mixed = sb("mixedF", [P, DM])
        inT = sb("inT", [P, KD, P])
        qs = sb("qs", [P, QW])
        qT = sb("qT_F", [P, KD, P])
        junk = sb("junkF", [P, DM], mybir.dt.bfloat16)
        tmp = sb("tmpF", [P, DM])
        u_rows = sb("u_rows", [P, RU, DM])
        v_rows = sb("v_rows", [P, RV, DM])
        diag = sb("diag", [P, RD, P])
        stat = sb("stat", [P, 2])
        iota_i = sb("iota_i", [P, TOPK], u32)
        iota16 = sb("iota16", [P, TOPK])
        best = sb("best", [P, 2, TOPK])
        where = sb("where", [P, 2, TOPK], u32)
        where_f = sb("where_f", [P, 2, TOPK])
        rest = sb("rest", [P, NKEYS])
        cand = sb("cand", [P, TOPK, TOPK])
        cand2 = sb("cand2", [P, TOPK * TOPK])
        pos = sb("pos", [P, TOPK], u32)
        pos2 = sb("pos2", [P, 2, TOPK], u32)
        pos_f = sb("pos_f", [P, 2, TOPK])
        hit = sb("hit", [P, TOPK, TOPK])
        e_f = sb("e_f", [P, 2, TOPK])
        top = sb("top", [P, PEER_HEADS, TOPK])
        gates = sb("gatesF", [P, 2, PEER_HEADS, TOPK])
        gsum = sb("gsum", [P, PEER_HEADS])
        idx = sb("idx", [P, RI, PICKS], u32)
        dots = sb("dots", [P, PICKS])
        weight = sb("weight", [P, PICKS])
        acc = banks(ctx, "acc", 2)
        ps_A = banks(ctx, "ps_A", 2)
        ps_B = banks(ctx, "ps_B", 2)
        ps_C = banks(ctx, "ps_C", 2)

        s_wo, s_wq, s_keys, s_rows, s_mix = sem("f_wo"), sem("f_wq"), sem("f_keys"), sem("f_rows"), sem("f_mix")
        s_h = [sem(f"f_h{i}") for i in range(RH)]
        s_u = [sem(f"f_u{i}") for i in range(RU)]
        s_v = [sem(f"f_v{i}") for i in range(RV)]
        iota_done, iota_ready, gain_done, keys_mm, keys_ev = (
            sem("f_iota"), sem("f_iota16"), sem("f_gain"), sem("f_keysmm"), sem("f_keysev"))
        step_mm, step_ev, h_done, mean_done, root_done, n2_done, topk_done = (
            sem("f_step"), sem("f_ev"), sem("f_hd"), sem("f_mean"), sem("f_root"), sem("f_n2"), sem("f_topk"))
        u_used, v_used, diag_done, act_done, weight_done, shifted, exp_done = (
            sem("f_uused"), sem("f_vused"), sem("f_diag"), sem("f_act"), sem("f_weight"), sem("f_shift"), sem("f_exp"))
        acc_read, fin_mean, fin_root, fin_done, chain = (
            sem("f_accread"), sem("f_fmean"), sem("f_froot"), sem("f_fin"), sem("f_chain"))

        STEPS = ("mixT", "project", "n2T", "query0", "query1", "qT0", "score0", "qT1", "score1")
        BANKS = dict(mixT=ps_A, project=ps_B, n2T=ps_A, query0=ps_C, query1=ps_B, qT0=ps_A, score0=ps_C, qT1=ps_B, score1=ps_A)
        EVACS = tuple(s for s in STEPS if s != "project")
        PE_SLOT = dict(mixT=4, project=8, n2T=26, query0=30, query1=36, qT0=42, score0=46, qT1=50, score1=54)
        H_SLOT, ROOT_SLOT, N_SLOT, TOPK_SLOT = 14, 18, 20, 58
        PHASES = range(-1, TT + 2)

        def steps_done(t, name):
            return len(STEPS) * t + STEPS.index(name) + 1

        def evacs_done(t, name):
            return len(EVACS) * t + EVACS.index(name) + 1

        with nc.Block() as block:
            @block.sync
            def _(sp):
                def load_mixed(t):
                    sp.dma_start(mixed[:, :], mix_scr[t * P:(t + 1) * P, :]).then_inc(s_mix, 16)

                def load_x(t):
                    sp.dma_start(h[:, t % RH, :], a["x"][0, t * P:(t + 1) * P, :]).then_inc(s_h[t % RH], 16)

                load_mixed(0)
                load_x(0)
                sp.dma_start(w_out[:, :, :], a["w_out"][0].rearrange("(k p) n -> p k n", p=P)).then_inc(s_wo, 16)
                for i, row in enumerate((gate1, shift2, gain2, gate2)):
                    sp.dma_start(row[:, :], mod_scr[(2 + i) * DM:(3 + i) * DM].partition_broadcast(P)).then_inc(s_rows, 16)
                sp.dma_start(tmp[:, :], a["norm2_g"][0].partition_broadcast(P)).then_inc(s_rows, 16)
                sp.dma_start(final_g[:, :], a["final_g"].partition_broadcast(P)).then_inc(s_rows, 16)
                sp.dma_start(keys[:, :, :], a["peer_keys"][0].rearrange("z n d -> n z d")).then_inc(s_keys, 16)
                sp.dma_start(w_q[:, :, :], a["peer_wq"][0].rearrange("(k p) n -> p k n", p=P)).then_inc(s_wq, 16)
                for i in PHASES:
                    t = i - 2
                    if 0 <= t:
                        sp.wait_ge(fin_done, t + 1)
                        sp.dma_start(out[0, t * P:(t + 1) * P, :], tmp[:, :]).then_inc(s_out, 16)
                    t = i + 2
                    if 1 <= t < TT:
                        sp.wait_ge(step_mm, steps_done(t - 1, "mixT"))
                        load_mixed(t)
                        if t >= RH:
                            sp.wait_ge(fin_done, t - RH + 1)
                        load_x(t)
                sp.wait_ge(s_out, 16 * TT)

            @block.gpsimd
            def _(pool):
                nc.gpsimd.iota(iota_i[:, :], pattern=[[1, TOPK]], base=0, channel_multiplier=0).then_inc(iota_done, 1)

                def gather(table, ring, r, t, j, done):
                    pool.indirect_dma_start(ring[:, r, :], None, table,
                                            bass.IndirectOffsetOnAxis(ap=idx[:, t % RI, j:j + 1], axis=0)).then_inc(done, 16)

                for i in range(TT + 1):
                    for j in range(PICKS):
                        if j == 0 and i < TT:
                            pool.wait_ge(topk_done, i + 1)
                        if i >= 1:
                            n = (i - 1) * PICKS + j
                            if n >= RV:
                                pool.wait_ge(v_used, n - RV + 1)
                            gather(a["peer_v"][0], v_rows, n % RV, i - 1, j, s_v[n % RV])
                        if i < TT:
                            n = i * PICKS + j
                            if n >= RU:
                                pool.wait_ge(u_used, n - RU + 1)
                            gather(a["peer_u"][0], u_rows, n % RU, i, j, s_u[n % RU])

            @block.scalar
            def _(act):
                act.wait_ge(keys_mm, 1)
                nc.scalar.activation(keysT[:, :, :], ps_C[:, 0:2 * P].rearrange("p (z n) -> p z n", z=2), ACT.Copy).then_inc(keys_ev, 1)

                def evacuate(t, name):
                    act.wait_ge(step_mm, steps_done(t, name))
                    src = BANKS[name]
                    if name in ("mixT", "n2T"):
                        dst = inT[:, :, :].rearrange("p k n -> p (k n)")
                    elif name in ("qT0", "qT1"):
                        dst = qT[:, :, :].rearrange("p k n -> p (k n)")
                    else:
                        half = int(name[-1])
                        dst = qs[:, half * DM:(half + 1) * DM]
                        if name == "query0" and t:
                            act.wait_ge(topk_done, t)
                    nc.scalar.activation(dst, src[:, :], ACT.Copy).then_inc(step_ev, 1)

                events = {PE_SLOT[s] + 2 + 2 * (s in ("query0", "query1")): s for s in EVACS}
                for i in PHASES:
                    t = i + 1
                    for j in range(PICKS):
                        if 1 <= i <= TT:
                            n = (i - 1) * PICKS + j
                            if j == 0:
                                act.wait_ge(weight_done, i)
                            if n >= RD:
                                act.wait_ge(v_used, n - RD + 1)
                            nc.scalar.activation(diag[:, n % RD, :], ident[:, :], ACT.Copy, scale=weight[:, j:j + 1]).then_inc(diag_done, 1)
                        if j == 2 and i >= 2:
                            act.wait_ge(fin_mean, i - 1)
                            nc.scalar.activation(stat[:, 1:2], stat[:, 1:2], ACT.Sqrt).then_inc(fin_root, 1)
                        if t < TT:
                            if j in events:
                                evacuate(t, events[j])
                            if j == ROOT_SLOT:
                                act.wait_ge(mean_done, t + 1)
                                nc.scalar.activation(stat[:, 0:1], stat[:, 0:1], ACT.Sqrt).then_inc(root_done, 1)
                    if t < TT:
                        act.wait_ge(shifted, t + 1)
                        g = gates[:, t % 2, :, :]
                        nc.scalar.activation(g, g, ACT.Exp).then_inc(exp_done, 1)
                    if 0 <= i < TT:
                        act.wait_ge(u_used, (i + 1) * PICKS)
                        nc.scalar.activation(dots[:, :], dots[:, :], ACT.Gelu).then_inc(act_done, 1)

            @block.vector
            def _(v):
                links = [0]

                def link(ins):
                    links[0] += 1
                    ins.then_inc(chain, 1)
                    v.wait_ge(chain, links[0])

                v.wait_ge(iota_done, 1)
                link(nc.vector.tensor_copy(iota16[:, :], iota_i[:, :]))
                v.wait_ge(s_rows, 96)
                link(nc.vector.scalar_tensor_tensor(out=gain2[:, :], in0=gain2[:, :], scalar=1.0, in1=tmp[:, :], op0=ALU.add, op1=ALU.mult))

                def residual(t):
                    ht = h[:, t % RH, :]
                    v.wait_ge(step_mm, steps_done(t, "project"))
                    link(nc.vector.tensor_tensor(n2[:, t % 2, :], ps_B[:, :], gate1[:, :], ALU.mult))
                    v.wait_ge(s_h[t % RH], 16 * (t // RH + 1))
                    nc.vector.tensor_tensor(ht, ht, n2[:, t % 2, :], ALU.add).then_inc(h_done, 1)
                    v.wait_ge(h_done, t + 1)
                    link(nc.vector.tensor_tensor_reduce(out=junk[:, :], in0=ht, in1=ht, scale=1.0, scalar=0.0, op0=ALU.mult, op1=ALU.add,
                                                        accum_out=stat[:, 0:1]))
                    nc.vector.tensor_scalar(stat[:, 0:1], stat[:, 0:1], 1.0 / DM, EPS, ALU.mult, ALU.add).then_inc(mean_done, 1)

                def second_norm(t):
                    v.wait_ge(root_done, t + 1)
                    link(nc.vector.reciprocal(stat[:, 0:1], stat[:, 0:1]))
                    link(nc.vector.scalar_tensor_tensor(out=n2[:, t % 2, :], in0=h[:, t % RH, :], scalar=stat[:, 0:1], in1=gain2[:, :],
                                                        op0=ALU.mult, op1=ALU.mult))
                    nc.vector.tensor_tensor(n2[:, t % 2, :], n2[:, t % 2, :], shift2[:, :], ALU.add).then_inc(n2_done, 1)
                    v.wait_ge(n2_done, t + 1)

                def top16(values, spare, val, ind):
                    link(nc.vector.max(val[:, 0:8], values))
                    link(nc.vector.max_index(ind[:, 0:8], val[:, 0:8], values))
                    link(nc.vector.match_replace(spare, val[:, 0:8], values, LOWEST))
                    link(nc.vector.max(val[:, 8:16], spare))
                    link(nc.vector.max_index(ind[:, 8:16], val[:, 8:16], spare))

                def route(t, hd):
                    if hd == 0:
                        v.wait_ge(step_ev, evacs_done(t, "score1"))
                    for z in range(2):
                        b = 2 * hd + z
                        top16(qs[:, b * P:(b + 1) * P], rest[:, :], best[:, z, :], where[:, z, :])
                    link(nc.vector.tensor_copy(where_f[:, :, :], where[:, :, :]))
                    link(nc.vector.tensor_tensor(cand[:, :, :], best[:, 0, :].unsqueeze(2).broadcast_to([P, TOPK, TOPK]),
                                                 best[:, 1, :].unsqueeze(1).broadcast_to([P, TOPK, TOPK]), ALU.add))
                    top16(cand[:, :, :].rearrange("p a b -> p (a b)"), cand2[:, :], top[:, hd, :], pos[:, :])
                    link(nc.vector.tensor_scalar(pos2[:, 0, :], pos[:, :], 4, None, ALU.logical_shift_right))
                    link(nc.vector.tensor_scalar(pos2[:, 1, :], pos[:, :], TOPK - 1, None, ALU.bitwise_and))
                    link(nc.vector.tensor_copy(pos_f[:, :, :], pos2[:, :, :]))
                    for z in range(2):
                        link(nc.vector.tensor_tensor(hit[:, :, :], iota16[:, :].unsqueeze(1).broadcast_to([P, TOPK, TOPK]),
                                                     pos_f[:, z, :].unsqueeze(2).broadcast_to([P, TOPK, TOPK]), ALU.is_equal))
                        link(nc.vector.tensor_tensor(hit[:, :, :], hit[:, :, :], where_f[:, z, :].unsqueeze(1).broadcast_to([P, TOPK, TOPK]),
                                                     ALU.mult))
                        link(nc.vector.tensor_reduce(e_f[:, z, :], hit[:, :, :], AX.X, ALU.add))
                    if t >= RI:
                        v.wait_ge(v_used, (t - RI + 1) * PICKS)
                    ins = nc.vector.scalar_tensor_tensor(out=idx[:, t % RI, hd * TOPK:(hd + 1) * TOPK], in0=e_f[:, 0, :],
                                                         scalar=float(NKEYS), in1=e_f[:, 1, :], op0=ALU.mult, op1=ALU.add)
                    if hd < PEER_HEADS - 1:
                        link(ins)
                        return
                    ins.then_inc(topk_done, 1)
                    v.wait_ge(topk_done, t + 1)
                    if t >= 2:
                        v.wait_ge(weight_done, t - 1)
                    nc.vector.tensor_tensor(gates[:, t % 2, :, :], top[:, :, :], top[:, :, 0:1].broadcast_to([P, PEER_HEADS, TOPK]),
                                            ALU.subtract).then_inc(shifted, 1)

                def softmax(t):
                    v.wait_ge(exp_done, t + 1)
                    g = gates[:, t % 2, :, :]
                    link(nc.vector.tensor_reduce(gsum[:, :], g, AX.X, ALU.add))
                    link(nc.vector.reciprocal(gsum[:, :], gsum[:, :]))
                    link(nc.vector.tensor_tensor(g, g, gsum[:, :].unsqueeze(2).broadcast_to([P, PEER_HEADS, TOPK]), ALU.mult))

                def finish_sum(t):
                    ht = h[:, t % RH, :]
                    v.wait_ge(v_used, (t + 1) * PICKS)
                    if t:
                        v.wait_ge(s_out, 16 * t)
                    nc.vector.tensor_tensor(tmp[:, :], acc[:, :], gate2[:, :], ALU.mult).then_inc(acc_read, 1)
                    v.wait_ge(acc_read, t + 1)
                    link(nc.vector.tensor_tensor(ht, ht, tmp[:, :], ALU.add))
                    link(nc.vector.tensor_tensor_reduce(out=junk[:, :], in0=ht, in1=ht, scale=1.0, scalar=0.0, op0=ALU.mult, op1=ALU.add,
                                                        accum_out=stat[:, 1:2]))
                    nc.vector.tensor_scalar(stat[:, 1:2], stat[:, 1:2], 1.0 / DM, EPS, ALU.mult, ALU.add).then_inc(fin_mean, 1)

                def finish_norm(t):
                    v.wait_ge(fin_root, t + 1)
                    link(nc.vector.reciprocal(stat[:, 1:2], stat[:, 1:2]))
                    nc.vector.scalar_tensor_tensor(out=tmp[:, :], in0=h[:, t % RH, :], scalar=stat[:, 1:2], in1=final_g[:, :],
                                                   op0=ALU.mult, op1=ALU.mult).then_inc(fin_done, 1)
                    v.wait_ge(fin_done, t + 1)

                for i in PHASES:
                    t = i + 1
                    for j in range(PICKS):
                        if i >= 2 and j == 0:
                            finish_sum(i - 2)
                        if i >= 2 and j == 4:
                            finish_norm(i - 2)
                        if 0 <= i < TT:
                            n = i * PICKS + j
                            v.wait_ge(s_u[n % RU], 16 * (n // RU + 1))
                            if j == 0 and i:
                                v.wait_ge(weight_done, i)
                            elif n:
                                v.wait_ge(u_used, n)
                            nc.vector.tensor_tensor_reduce(out=junk[:, :], in0=u_rows[:, n % RU, :], in1=n2[:, i % 2, :], scale=1.0, scalar=0.0,
                                                           op0=ALU.mult, op1=ALU.add, accum_out=dots[:, j:j + 1]).then_inc(u_used, 1)
                        if t < TT:
                            if j in (H_SLOT, N_SLOT) and 0 <= i:
                                v.wait_ge(u_used, i * PICKS + j + 1)
                            if j == H_SLOT:
                                residual(t)
                            if j == N_SLOT:
                                second_norm(t)
                            if j >= TOPK_SLOT and (j - TOPK_SLOT) % 8 == 0 and (j - TOPK_SLOT) // 8 < PEER_HEADS:
                                route(t, (j - TOPK_SLOT) // 8)
                    if t < TT:
                        softmax(t)
                    if 0 <= i < TT:
                        v.wait_ge(act_done, i + 1)
                        if i:
                            v.wait_ge(diag_done, i * PICKS)
                        nc.vector.tensor_tensor(weight[:, :], dots[:, :], gates[:, i % 2, :, :].rearrange("p h k -> p (h k)"),
                                                ALU.mult).then_inc(weight_done, 1)

            @block.tensor
            def _(pe):
                pe.wait_ge(s_keys, 16)
                for z in range(2):
                    last = nc.tensor.transpose(ps_C[:, z * P:(z + 1) * P], keys[:, z, :], ident[:, :])
                last.then_inc(keys_mm, 1)
                pe.wait_ge(keys_ev, 1)

                def transposes(bank, src, t, name):
                    for k in range(KD):
                        last = nc.tensor.transpose(bank[:, k * P:(k + 1) * P], src[:, k * P:(k + 1) * P], ident[:, :])
                    last.then_inc(step_mm, 1)

                def columns(bank, half, w, c0, t, name):
                    for k in range(KD):
                        last = nc.tensor.matmul(bank[:, half * HALF:(half + 1) * HALF], inT[:, k, :], w[:, k, c0:c0 + HALF],
                                                start=(k == 0), stop=(k == KD - 1))
                    if half:
                        last.then_inc(step_mm, 1)

                def run(t, name, part):
                    bank = BANKS[name]
                    if name == "mixT":
                        pe.wait_ge(s_mix, 16 * (t + 1))
                        if t:
                            pe.wait_ge(step_ev, evacs_done(t - 1, "score1"))
                        transposes(bank, mixed[:, :], t, name)
                    elif name == "project":
                        if part == 0:
                            pe.wait_ge(step_ev, evacs_done(t, "mixT"))
                            pe.wait_ge(s_wo, 16)
                        columns(bank, part, w_out, part * HALF, t, name)
                    elif name == "n2T":
                        pe.wait_ge(n2_done, t + 1)
                        transposes(bank, n2[:, t % 2, :], t, name)
                    elif name in ("query0", "query1"):
                        if part == 0:
                            pe.wait_ge(step_ev, evacs_done(t, "n2T"))
                            pe.wait_ge(h_done, t + 1)
                            pe.wait_ge(s_wq, 16)
                        columns(bank, part, w_q, int(name[-1]) * DM + part * HALF, t, name)
                    elif name in ("qT0", "qT1"):
                        half = int(name[-1])
                        pe.wait_ge(step_ev, evacs_done(t, "query1" if half == 0 else "score0"))
                        transposes(bank, qs[:, half * DM:(half + 1) * DM], t, name)
                    else:
                        half = int(name[-1])
                        pe.wait_ge(step_ev, evacs_done(t, "qT0" if half == 0 else "qT1"))
                        for b in range(KD):
                            last = nc.tensor.matmul(bank[:, b * P:(b + 1) * P], qT[:, b, :], keysT[:, b % 2, :], start=True, stop=True)
                        last.then_inc(step_mm, 1)

                events = {}
                for s in STEPS:
                    events[PE_SLOT[s]] = (s, 0)
                    if s in ("project", "query0", "query1"):
                        events[PE_SLOT[s] + 2] = (s, 1)
                for i in PHASES:
                    t = i + 1
                    for j in range(PICKS):
                        if 1 <= i <= TT:
                            n = (i - 1) * PICKS + j
                            pe.wait_ge(s_v[n % RV], 16 * (n // RV + 1))
                            pe.wait_ge(diag_done, n + 1)
                            if j == 0 and i >= 2:
                                pe.wait_ge(acc_read, i - 1)
                            for half in range(2):
                                last = nc.tensor.matmul(acc[:, half * HALF:(half + 1) * HALF], diag[:, n % RD, :],
                                                        v_rows[:, n % RV, half * HALF:(half + 1) * HALF],
                                                        start=(j == 0), stop=(j == PICKS - 1))
                            last.then_inc(v_used, 1)
                        if t < TT and j in events:
                            run(t, *events[j])


_INS = ["x", "c", "w_ada", "b_ada", "norm1_g", "w_in", "conv_w", "conv_b", "dt_bias_f", "dt_bias_b", "a_log_f", "a_log_b",
        "d_skip", "ssd_norm_g", "w_ssd_br", "na_rpb", "w_na_br", "w_out", "norm2_g", "peer_wq", "peer_keys", "peer_u",
        "peer_v", "final_g"]


def kernel(**inputs):
    import concourse.bacc as bacc
    from concourse.bass_utils import run_bass_kernel_spmd

    nc = bacc.Bacc("TRN2", target_bir_lowering=False, num_devices=1)
    arrays, args = {}, {}
    for name in _INS:
        arr = np.ascontiguousarray(inputs[name])
        arrays[f"in_{name}"] = arr
        args[name] = nc.dram_tensor(f"in_{name}", arr.shape, mybir.dt.from_np(arr.dtype), kind="ExternalInput").ap()
    out = nc.dram_tensor("out", (1, SEQ, DM), mybir.dt.float32, kind="ExternalOutput").ap()
    build_program(nc, args, out)
    r = run_bass_kernel_spmd(nc, [arrays], core_ids=[0])
    return r.results[0]["out"]
```

```python
import numpy as np
import concourse.bass as bass
from concourse import mybir
from contextlib import ExitStack

P = 128
SEQ, DM = 1024, 1024
TT = SEQ // P
KD = DM // P
HALF = 512
GRID_W, GRID_H = 64, SEQ // 64
EPS = 1e-6
SSD_HEADS, HEADDIM, GROUPS, HPG, STATE = 16, 64, 4, 4, 128
CONV_W = 5
D_XBC = DM + 2 * GROUPS * STATE
XBC_BLOCKS = D_XBC // P
NA_HEADS, NA_KH, NA_KW = 16, 8, 16
PAIRS = NA_HEADS // 2
COL_Z, COL_XBC = 0, DM
COL_DT = COL_XBC + D_XBC
COL_QKV = COL_DT + 2 * SSD_HEADS
COL_GATES = COL_QKV + 3 * DM
MODS = 6 * DM
BIAS_ROWS, BIAS_COLS = 17, 128
BIAS_PAD = 48
SLOTS = 16
MASKED = -1.0e30
PEER_HEADS, NKEYS, TOPK, DHALF = 8, 128, 16, 128
QW = PEER_HEADS * 2 * DHALF
PICKS = PEER_HEADS * TOPK
LOWEST = -3.0e38


def build_program(nc, a, out):
    f32, u32 = mybir.dt.float32, mybir.dt.uint32
    ALU, ACT, AX = mybir.AluOpType, mybir.ActivationFunctionType, mybir.AxisListType

    def scratch(name, shape):
        return nc.dram_tensor(name, shape, f32).ap()

    mod_scr = scratch("mod_scr", [MODS])
    rpb_scr = scratch("rpb_scr", [NA_HEADS, BIAS_ROWS, GRID_W, GRID_W])
    zg_scr = scratch("zg_scr", [3, SEQ, DM])
    na_scr = scratch("na_scr", [SEQ, DM])
    mix_scr = scratch("mix_scr", [SEQ, DM])
    w_in = a["w_in"][0].rearrange("(k p) n -> p k n", p=P)

    top = ExitStack()
    with top:
        def opener(ctx):
            def sb(name, shape, dt=f32):
                return ctx.enter_context(nc.sbuf_tensor(name, shape, dt))
            return sb

        def banks(ctx, name, n):
            return ctx.enter_context(nc.psum_tensor(name, [P, n * HALF], f32))

        stored = nc.alloc_semaphore(name="out_stored")
        held = []

        def sem(name):
            held.append(nc.alloc_semaphore(name=name))
            return held[-1]

        def retire_semaphores():
            nc.clear_and_free_semaphores(held)
            nc.all_engine_barrier()
            held.clear()

        sb = opener(top)
        ident = sb("ident", [P, P])

        mid = ExitStack()
        with mid:
            sbm = opener(mid)
            upto = sbm("upto", [P, P])
            since = sbm("since", [P, P])
            after = sbm("after", [P, P])
            before = sbm("before", [P, P])
            ones = sbm("ones", [P, P])
            X = sbm("X", [P, TT, DM])
            y_rstd = sbm("y_rstd", [P, TT])
            scan = ExitStack()
            with scan:
                sbs = opener(scan)
                BT = sbs("BT", [P, GROUPS, SEQ])
                CT = sbs("CT", [P, GROUPS, SEQ])
                dt = sbs("dt", [P, TT, 2 * SSD_HEADS])
                dA = sbs("dA", [P, TT, 2 * SSD_HEADS])
                front = ExitStack()
                with front:
                    n1T = opener(front)("n1T", [P, KD, SEQ])
                    cT = opener(front)("cT", [P, KD])
                    consts = (ident, upto, since, after, before, ones)
                    stage_condition(nc, a, opener, banks, sem, consts, X, n1T, cT, mod_scr)
                    stage_project(nc, a, opener, banks, sem, w_in, ident, n1T, cT, X, BT, CT, dt, dA, zg_scr, mod_scr, rpb_scr)
                    stage_attention(nc, a, opener, banks, sem, w_in, ident, n1T, rpb_scr, na_scr)
                retire_semaphores()
                stage_ssd(nc, a, opener, banks, sem, consts, X, BT, CT, dt, dA, zg_scr, y_rstd)
            stage_merge(nc, a, opener, banks, sem, ident, X, y_rstd, zg_scr, na_scr, mix_scr)
        retire_semaphores()
        stage_peer(nc, a, opener, banks, sem, ident, mod_scr, mix_scr, out, stored)


def stage_condition(nc, a, opener, banks, sem, consts, xs, n1T, cT, mod_scr):
    ALU, ACT = mybir.AluOpType, mybir.ActivationFunctionType
    ident, upto, since, after, before, ones = consts
    ROWS = 3 * KD
    ctx = ExitStack()
    with ctx:
        sb = opener(ctx)
        c_rows = sb("c_rows", [KD, P])
        c_act = sb("c_act", [KD, P])
        rows = sb("rowsA", [ROWS, P])
        cols = sb("colsA", [P, ROWS])
        ada = sb("ada", [P, 2, KD, DM])
        mods = sb("modsA", [P, 2 * KD])
        junk = sb("junkA", [P, 2, DM])
        sumsq = sb("sumsqA", [P, TT])
        rstd = sb("rstdA", [P, TT])
        ps_c = banks(ctx, "ps_c", 1)
        ps_mod = banks(ctx, "ps_mod", 1)
        ps_n = [banks(ctx, f"ps_n{i}", 2) for i in range(3)]

        s_small, s_x = sem("a_small"), [sem("a_x0"), sem("a_x1")]
        s_ada = [sem("a_ada0"), sem("a_ada1")]
        c_done, cps_done, cT_done, mm_done, const_zero, const_done = (
            sem("a_c"), sem("a_cps"), sem("a_cT"), sem("a_mm"), sem("a_cz"), sem("a_cd"))
        sq_done, mean_done, sqrt_done, rstd_done, scaled, mods_done, gain_done, tr_done, ev_act, ev_dve = (
            sem("a_sq"), sem("a_mean"), sem("a_sqrt"), sem("a_rstd"), sem("a_scaled"), sem("a_mods"), sem("a_gain"),
            sem("a_tr"), sem("a_evact"), sem("a_evdve"))

        with nc.Block() as block:
            @block.sync
            def _(sp):
                w_ada = a["w_ada"][0].rearrange("(k p) n -> p k n", p=P)
                x_v = a["x"][0].rearrange("(t p) d -> p t d", p=P)
                sp.dma_start(c_rows[:, :], a["c"].rearrange("a (k p) -> (a k) p", p=P)).then_inc(s_small, 16)
                sp.dma_start(rows[0:KD, :], a["norm1_g"][0].rearrange("(k p) -> k p", p=P)).then_inc(s_small, 16)
                sp.dma_start(rows[KD:, :], a["b_ada"][0, 0:2 * DM].rearrange("(r p) -> r p", p=P)).then_inc(s_small, 16)
                for i in range(2):
                    sp.dma_start(xs[:, 4 * i:4 * i + 4, :], x_v[:, 4 * i:4 * i + 4, :]).then_inc(s_x[i], 16)
                for i in range(2):
                    sp.dma_start(ada[:, i, :, :], w_ada[:, :, i * DM:(i + 1) * DM]).then_inc(s_ada[i], 16)

            @block.gpsimd
            def _(pool):
                nc.gpsimd.memset(ident[:, :], 0.0).then_inc(const_zero, 1)
                for m in (upto, since, after, before):
                    nc.gpsimd.memset(m[:, :], 1.0).then_inc(const_zero, 1)
                nc.gpsimd.memset(ones[:, :], 1.0)
                pool.wait_ge(const_zero, 5)
                nc.gpsimd.affine_select(out=ident[:, :], in_=ident[:, :], compare_op=ALU.not_equal, fill=1.0,
                                        base=0, pattern=[[-1, P]], channel_multiplier=1).then_inc(const_done, 1)
                for m, sign, op in ((upto, -1, ALU.is_ge), (since, 1, ALU.is_ge), (after, 1, ALU.is_gt), (before, -1, ALU.is_gt)):
                    nc.gpsimd.affine_select(out=m[:, :], in_=m[:, :], compare_op=op, fill=0.0, base=0,
                                            pattern=[[-sign, P]], channel_multiplier=sign).then_inc(const_done, 1)

            @block.scalar
            def _(act):
                act.wait_ge(s_small, 48)
                nc.scalar.activation(c_act[:, :], c_rows[:, :], ACT.Silu).then_inc(c_done, 1)
                act.wait_ge(cps_done, 1)
                nc.scalar.activation(cT[:, :], ps_c[:, 0:KD], ACT.Copy).then_inc(cT_done, 1)
                nc.scalar.activation(cols[:, :], ps_c[:, KD:KD + ROWS], ACT.Copy).then_inc(cT_done, 1)
                for t in range(TT):
                    act.wait_ge(s_x[t // 4], 16)
                    if t >= 2:
                        act.wait_ge(sq_done, t - 1)
                    nc.scalar.activation(junk[:, t % 2, :], xs[:, t, :], ACT.Square, accum_out=sumsq[:, t:t + 1]).then_inc(sq_done, 1)
                act.wait_ge(mean_done, 1)
                nc.scalar.activation(rstd[:, :], rstd[:, :], ACT.Sqrt).then_inc(sqrt_done, 1)
                act.wait_ge(gain_done, 1)
                for k in range(1, KD, 2):
                    act.wait_ge(tr_done, k + 1)
                    nc.scalar.activation(n1T[:, k, :], ps_n[k % 3][:, :], ACT.Identity, bias=mods[:, k:k + 1],
                                         scale=mods[:, KD + k:KD + k + 1]).then_inc(ev_act, 1)

            @block.vector
            def _(v):
                v.wait_ge(sq_done, TT)
                nc.vector.tensor_scalar(rstd[:, :], sumsq[:, :], 1.0 / DM, EPS, ALU.mult, ALU.add).then_inc(mean_done, 1)
                v.wait_ge(sqrt_done, 1)
                nc.vector.reciprocal(rstd[:, :], rstd[:, :]).then_inc(rstd_done, 1)
                v.wait_ge(rstd_done, 1)
                for t in range(TT):
                    nc.vector.tensor_scalar(xs[:, t, :], xs[:, t, :], rstd[:, t:t + 1], None, ALU.mult).then_inc(scaled, 1)
                v.wait_ge(cT_done, 2)
                v.wait_ge(mm_done, 2)
                nc.vector.tensor_tensor(mods[:, :], ps_mod[:, 0:2 * KD], cols[:, KD:ROWS], ALU.add).then_inc(mods_done, 1)
                v.wait_ge(mods_done, 1)
                nc.vector.scalar_tensor_tensor(out=mods[:, KD:], in0=mods[:, KD:], scalar=1.0, in1=cols[:, 0:KD],
                                               op0=ALU.add, op1=ALU.mult).then_inc(gain_done, 1)
                v.wait_ge(gain_done, 1)
                for k in range(0, KD, 2):
                    v.wait_ge(tr_done, k + 1)
                    nc.vector.tensor_scalar(n1T[:, k, :], ps_n[k % 3][:, :], mods[:, KD + k:KD + k + 1], mods[:, k:k + 1],
                                            ALU.mult, ALU.add).then_inc(ev_dve, 1)

            @block.tensor
            def _(pe):
                pe.wait_ge(const_done, 1)
                pe.wait_ge(c_done, 1)
                nc.tensor.transpose(ps_c[:, 0:KD], c_act[:, :], ident[0:KD, 0:KD])
                nc.tensor.transpose(ps_c[:, KD:KD + ROWS], rows[:, :], ident[0:ROWS, 0:ROWS]).then_inc(cps_done, 1)
                pe.wait_ge(cT_done, 1)
                for q in range(2):
                    pe.wait_ge(s_ada[q], 16)
                    for cb in range(KD):
                        for k in range(KD):
                            last = nc.tensor.matmul(ps_mod[:, q * KD + cb:q * KD + cb + 1], ada[:, q, k, cb * P:(cb + 1) * P],
                                                    cT[:, k:k + 1], start=(k == 0), stop=(k == KD - 1))
                    last.then_inc(mm_done, 1)
                pe.wait_ge(scaled, TT)
                for k in range(KD):
                    if k >= 3:
                        o = k - 3
                        pe.wait_ge(ev_act if o % 2 else ev_dve, o // 2 + 1)
                    for t in range(TT):
                        last = nc.tensor.transpose(ps_n[k % 3][:, t * P:(t + 1) * P], xs[:, t, k * P:(k + 1) * P], ident[:, :])
                    last.then_inc(tr_done, 1)


def stage_project(nc, a, opener, banks, sem, w_in, ident, n1T, cT, X, BT, CT, dt, dA, zg_scr, mod_scr, rpb_scr):
    f32 = mybir.dt.float32
    ALU, ACT = mybir.AluOpType, mybir.ActivationFunctionType
    NH2 = 2 * SSD_HEADS
    ZB = 6
    z_cols = [COL_Z, COL_Z + HALF] + [COL_GATES + i * HALF for i in range(4)]
    RW, RZ, RS = 3, 2, 4
    ctx = ExitStack()
    with ctx:
        sb = opener(ctx)
        w_x = sb("w_x", [P, RW, KD, P])
        w_z = sb("w_z", [P, RZ, KD, HALF])
        w_dt = sb("w_dt", [P, KD, NH2])
        taps_rows = sb("taps_rows", [(CONV_W + 1) * XBC_BLOCKS, P])
        taps = sb("taps", [P, CONV_W + 1, XBC_BLOCKS])
        padded = sb("padded", [P, 2, SEQ + CONV_W - 1])
        conv = sb("conv", [P, 2, SEQ])
        xT = sb("xT", [P, 2, SEQ])
        staged = sb("staged", [P, RS, HALF])
        dt_bias = sb("dt_bias", [P, NH2])
        a_exp = sb("a_exp", [P, NH2])
        neg = sb("neg", [P, TT, NH2])
        ps_x = [banks(ctx, f"ps_x{i}", 2) for i in range(2)]
        ps_t = banks(ctx, "ps_t", 2)
        ps_dt = banks(ctx, "ps_dt", 1)
        AC = 4 * DM // XBC_BLOCKS
        MB = 4 * DM // P
        ada = sb("adaB", [P, 2, KD, AC])
        mod_cols = sb("mod_colsB", [P, MB])
        mod_rows = sb("mod_rowsB", [MB, P])
        b_ada = sb("b_adaB", [MB, P])
        bias_pad = sb("bias_pad", [NA_HEADS, BIAS_ROWS, BIAS_COLS])
        ps_mod = banks(ctx, "ps_modB", 1)
        s_ada = [sem("b_ada0"), sem("b_ada1")]
        s_pad, s_padw, pad_zero, s_modw = sem("b_pad"), sem("b_padw"), sem("b_padz"), sem("b_modw")
        ada_mm, cols_done, rows_ps, rows_done = sem("b_adamm"), sem("b_cols"), sem("b_rowsps"), sem("b_rows")

        s_small = sem("b_small")
        s_wx = [sem(f"b_wx{i}") for i in range(RW)]
        s_wz = [sem(f"b_wz{i}") for i in range(RZ)]
        s_st = [sem(f"b_st{i}") for i in range(RS)]
        taps_ps, taps_done, edge_done = sem("b_tapsps"), sem("b_taps"), sem("b_edge")
        x_mm, x_ev, conv_done, silu_done, xt_mm, xt_ev, chain = (
            sem("b_xmm"), sem("b_xev"), sem("b_conv"), sem("b_silu"), sem("b_xtmm"), sem("b_xtev"), sem("b_chain"))
        dt_mm, dt_act, z_mm, z_act = sem("b_dtmm"), sem("b_dtact"), sem("b_zmm"), sem("b_zact")

        with nc.Block() as block:
            @block.sync
            def _(sp):
                def load_x(b):
                    sp.dma_start(w_x[:, b % RW, :, :], w_in[:, :, COL_XBC + b * P:COL_XBC + (b + 1) * P]).then_inc(s_wx[b % RW], 16)

                def load_z(n):
                    sp.dma_start(w_z[:, n % RZ, :, :], w_in[:, :, z_cols[n]:z_cols[n] + HALF]).then_inc(s_wz[n % RZ], 16)

                def load_ada(b):
                    c0 = 2 * DM + b * AC
                    sp.dma_start(ada[:, b % 2, :, :], w_ada[:, :, c0:c0 + AC]).then_inc(s_ada[b % 2], 16)

                w_ada = a["w_ada"][0].rearrange("(k p) n -> p k n", p=P)
                load_x(0)
                sp.dma_start(taps_rows[0:CONV_W * XBC_BLOCKS, :], a["conv_w"][0].rearrange("w (b p) -> (w b) p", p=P)).then_inc(s_small, 16)
                sp.dma_start(taps_rows[CONV_W * XBC_BLOCKS:, :], a["conv_b"][0].rearrange("(b p) -> b p", p=P)).then_inc(s_small, 16)
                sp.dma_start(dt_bias[:, 0:SSD_HEADS], a["dt_bias_f"][0].partition_broadcast(P)).then_inc(s_small, 16)
                sp.dma_start(dt_bias[:, SSD_HEADS:], a["dt_bias_b"][0].partition_broadcast(P)).then_inc(s_small, 16)
                sp.dma_start(a_exp[:, 0:SSD_HEADS], a["a_log_f"][0].partition_broadcast(P)).then_inc(s_small, 16)
                sp.dma_start(a_exp[:, SSD_HEADS:], a["a_log_b"][0].partition_broadcast(P)).then_inc(s_small, 16)
                sp.dma_start(w_dt[:, :, :], w_in[:, :, COL_DT:COL_DT + NH2]).then_inc(s_small, 16)
                load_ada(0)
                load_x(1)
                load_ada(1)
                load_x(2)
                sp.dma_start(b_ada[:, :], a["b_ada"][0, 2 * DM:].rearrange("(r p) -> r p", p=P)).then_inc(s_modw, 16)
                for b in range(2, XBC_BLOCKS):
                    sp.wait_ge(ada_mm, b - 1)
                    load_ada(b)
                    if b + 1 < XBC_BLOCKS:
                        load_x(b + 1)
                load_z(0)
                load_z(1)
                sp.wait_ge(rows_done, 1)
                sp.dma_start(mod_scr[2 * DM:].rearrange("(r p) -> r p", p=P), mod_rows[:, :]).then_inc(s_modw, 16)
                sp.wait_ge(s_modw, 32)
                for n in range(ZB):
                    for t in range(TT):
                        m = n * TT + t
                        sp.wait_ge(z_act, m + 1)
                        sp.dma_start(zg_scr[n // 2, t * P:(t + 1) * P, (n % 2) * HALF:(n % 2 + 1) * HALF],
                                     staged[:, m % RS, :]).then_inc(s_st[m % RS], 16)
                    if n + RZ < ZB:
                        sp.wait_ge(z_mm, (n + 1) * TT)
                        load_z(n + RZ)
                for r in range(RS):
                    sp.wait_ge(s_st[r], 16 * (ZB * TT // RS))

            @block.gpsimd
            def _(pool):
                nc.gpsimd.memset(padded[:, :, 0:2], 0.0).then_inc(edge_done, 1)
                nc.gpsimd.memset(padded[:, :, SEQ + 2:SEQ + 4], 0.0).then_inc(edge_done, 1)
                nc.gpsimd.memset(bias_pad[:, :, :], 0.0).then_inc(pad_zero, 1)
                pool.wait_ge(pad_zero, 1)
                pool.dma_start(bias_pad[:, 1:16, BIAS_PAD:BIAS_PAD + 31], a["na_rpb"][0]).then_inc(s_pad, 16)
                pool.wait_ge(s_pad, 16)
                for r in range(BIAS_ROWS):
                    whole = bias_pad[:, r, :]
                    skewed = bass.AP(whole.tensor, whole.offset + BIAS_PAD + NA_KW - 1, [list(whole.ap[0]), [-1, GRID_W], [1, GRID_W]])
                    pool.dma_start(rpb_scr[:, r, :, :], skewed).then_inc(s_padw, 16)
                pool.wait_ge(s_padw, 16 * BIAS_ROWS)

            def gate(act, m, func):
                act.wait_ge(z_mm, m + 1)
                if m >= RS:
                    act.wait_ge(s_st[m % RS], 16 * (m // RS))
                nc.scalar.activation(staged[:, m % RS, :], ps_x[m % 2][:, 0:HALF], func).then_inc(z_act, 1)

            conv_chain = sem("b_convchain")

            @block.scalar
            def _(act):
                act.wait_ge(s_small, 112)
                act.wait_ge(taps_ps, 1)
                nc.scalar.activation(taps[:, :, :], ps_dt[:, 0:(CONV_W + 1) * XBC_BLOCKS].rearrange("p (w b) -> p w b", w=CONV_W + 1),
                                     ACT.Copy).then_inc(taps_done, 1)
                for b in range(XBC_BLOCKS + 2):
                    if b < XBC_BLOCKS:
                        act.wait_ge(x_mm, b + 1)
                        if b >= 2:
                            act.wait_ge(conv_done, b - 1)
                        nc.scalar.activation(padded[:, b % 2, 2:SEQ + 2], ps_x[b % 2][:, :], ACT.Copy).then_inc(x_ev, 1)
                    s = b - 1
                    if 0 <= s < XBC_BLOCKS:
                        act.wait_ge(taps_done, 1)
                        act.wait_ge(conv_done, s + 1)
                        if 2 <= s < 8:
                            act.wait_ge(xt_mm, s - 1)
                        dst = xT[:, s % 2, :] if s < 8 else (BT if s < 12 else CT)[:, s % 4, :]
                        nc.scalar.activation(dst, conv[:, s % 2, :], ACT.Silu, bias=taps[:, CONV_W, s:s + 1]).then_inc(silu_done, 1)
                    r = b - 2
                    if 0 <= r < 8:
                        act.wait_ge(xt_mm, r + 1)
                        nc.scalar.activation(X[:, :, r * P:(r + 1) * P], ps_t[:, :].rearrange("p (t n) -> p t n", t=TT), ACT.Copy).then_inc(xt_ev, 1)
                for m in range(2 * TT):
                    gate(act, m, ACT.Silu)
                for m in range(2 * TT, ZB * TT):
                    gate(act, m, ACT.Sigmoid)
                act.wait_ge(dt_act, 1)
                nc.scalar.activation(neg[:, :, :], neg[:, :, :], ACT.Exp).then_inc(chain, 1)
                nc.scalar.activation(a_exp[:, :], a_exp[:, :], ACT.Exp).then_inc(chain, 1)
                act.wait_ge(chain, 2)
                nc.scalar.activation(neg[:, :, :], neg[:, :, :], ACT.Ln, bias=1.0).then_inc(chain, 1)

            @block.vector
            def _(v):
                links = 0
                v.wait_ge(edge_done, 2)
                v.wait_ge(taps_done, 1)
                for b in range(XBC_BLOCKS):
                    v.wait_ge(x_ev, b + 1)
                    if b >= 2:
                        v.wait_ge(silu_done, b - 1)
                    nc.vector.tensor_scalar(conv[:, b % 2, :], padded[:, b % 2, 0:SEQ], taps[:, 0, b:b + 1], None,
                                            ALU.mult).then_inc(conv_chain, 1)
                    links += 1
                    for w in range(1, CONV_W):
                        v.wait_ge(conv_chain, links)
                        step = nc.vector.scalar_tensor_tensor(out=conv[:, b % 2, :], in0=padded[:, b % 2, w:w + SEQ],
                                                              scalar=taps[:, w, b:b + 1], in1=conv[:, b % 2, :],
                                                              op0=ALU.mult, op1=ALU.add)
                        if w < CONV_W - 1:
                            step.then_inc(conv_chain, 1)
                            links += 1
                    step.then_inc(conv_done, 1)
                v.wait_ge(ada_mm, XBC_BLOCKS)
                nc.vector.tensor_copy(mod_cols[:, :], ps_mod[:, 0:MB]).then_inc(cols_done, 1)
                v.wait_ge(rows_ps, 1)
                v.wait_ge(s_modw, 16)
                nc.vector.tensor_tensor(mod_rows[:, :], ps_t[0:MB, 0:P], b_ada[:, :], ALU.add).then_inc(rows_done, 1)
                v.wait_ge(dt_mm, 1)
                v.wait_ge(s_small, 112)
                nc.vector.tensor_tensor(dt[:, :, :], ps_dt[:, 0:TT * NH2].rearrange("p (t h) -> p t h", t=TT),
                                        dt_bias[:, :].unsqueeze(1).broadcast_to([P, TT, NH2]), ALU.add).then_inc(conv_chain, 1)
                v.wait_ge(conv_chain, links + 1)
                nc.vector.tensor_scalar(neg[:, :, :], dt[:, :, :], -1.0, None, ALU.mult).then_inc(conv_chain, 1)
                v.wait_ge(conv_chain, links + 2)
                nc.vector.tensor_tensor(neg[:, :, :], neg[:, :, :], dt[:, :, :], ALU.min).then_inc(dt_act, 1)
                v.wait_ge(chain, 3)
                nc.vector.scalar_tensor_tensor(out=dt[:, :, :], in0=dt[:, :, :], scalar=0.0, in1=neg[:, :, :],
                                               op0=ALU.max, op1=ALU.add).then_inc(conv_chain, 1)
                v.wait_ge(conv_chain, links + 3)
                nc.vector.scalar_tensor_tensor(out=dA[:, :, :], in0=dt[:, :, :], scalar=-1.0,
                                               in1=a_exp[:, :].unsqueeze(1).broadcast_to([P, TT, NH2]),
                                               op0=ALU.mult, op1=ALU.mult).then_inc(dt_act, 1)

            @block.tensor
            def _(pe):
                pe.wait_ge(s_small, 112)
                nc.tensor.transpose(ps_dt[:, 0:(CONV_W + 1) * XBC_BLOCKS], taps_rows[:, :],
                                    ident[0:(CONV_W + 1) * XBC_BLOCKS, 0:(CONV_W + 1) * XBC_BLOCKS]).then_inc(taps_ps, 1)
                for b in range(XBC_BLOCKS + 2):
                    if b < XBC_BLOCKS:
                        pe.wait_ge(s_wx[b % RW], 16 * (b // RW + 1))
                        if b >= 2:
                            pe.wait_ge(x_ev, b - 1)
                        for h in range(2):
                            for k in range(KD):
                                last = nc.tensor.matmul(ps_x[b % 2][:, h * HALF:(h + 1) * HALF], w_x[:, b % RW, k, :],
                                                        n1T[:, k, h * HALF:(h + 1) * HALF], start=(k == 0), stop=(k == KD - 1))
                        last.then_inc(x_mm, 1)
                        pe.wait_ge(s_ada[b % 2], 16 * (b // 2 + 1))
                        for cb in range(AC // P):
                            n = b * (AC // P) + cb
                            for k in range(KD):
                                last = nc.tensor.matmul(ps_mod[:, n:n + 1], ada[:, b % 2, k, cb * P:(cb + 1) * P], cT[:, k:k + 1],
                                                        start=(k == 0), stop=(k == KD - 1))
                        last.then_inc(ada_mm, 1)
                    r = b - 2
                    if 0 <= r < 8:
                        pe.wait_ge(silu_done, r + 1)
                        if r:
                            pe.wait_ge(xt_ev, r)
                        for t in range(TT):
                            last = nc.tensor.transpose(ps_t[:, t * P:(t + 1) * P], xT[:, r % 2, t * P:(t + 1) * P], ident[:, :])
                        last.then_inc(xt_mm, 1)
                pe.wait_ge(xt_ev, 8)
                pe.wait_ge(cols_done, 1)
                nc.tensor.transpose(ps_t[0:MB, 0:P], mod_cols[:, :], ident[:, :]).then_inc(rows_ps, 1)
                pe.wait_ge(taps_done, 1)
                for t in range(TT):
                    for k in range(KD):
                        last = nc.tensor.matmul(ps_dt[:, t * NH2:(t + 1) * NH2], n1T[:, k, t * P:(t + 1) * P], w_dt[:, k, :],
                                                start=(k == 0), stop=(k == KD - 1))
                last.then_inc(dt_mm, 1)
                for m in range(ZB * TT):
                    n, t = divmod(m, TT)
                    pe.wait_ge(s_wz[n % RZ], 16 * (n // RZ + 1))
                    if m < 2:
                        pe.wait_ge(x_ev, XBC_BLOCKS)
                    else:
                        pe.wait_ge(z_act, m - 1)
                    for k in range(KD):
                        last = nc.tensor.matmul(ps_x[m % 2][:, 0:HALF], n1T[:, k, t * P:(t + 1) * P], w_z[:, n % RZ, k, :],
                                                start=(k == 0), stop=(k == KD - 1))
                    last.then_inc(z_mm, 1)


def stage_attention(nc, a, opener, banks, sem, w_in, ident, n1T, rpb_scr, na_scr):
    f32 = mybir.dt.float32
    ALU, ACT, AX = mybir.AluOpType, mybir.ActivationFunctionType, mybir.AxisListType
    UPP = 2 * TT
    UNITS = PAIRS * UPP
    SPAN = NA_KH * GRID_W + GRID_W
    first_row = [min(max(2 * j - NA_KH // 2, 0), GRID_H - NA_KH) for j in range(TT)]
    inner = [0 < 2 * j + 1 - NA_KH // 2 <= GRID_H - NA_KH and 2 * j - NA_KH // 2 >= 0 for j in range(TT)]
    width = [SPAN if inner[j] else SPAN - GRID_W for j in range(TT)]
    slot0 = [first_row[j] - 2 * j + NA_KH - 1 for j in range(TT)]
    GROUP = (("v", 0), ("v", 1), ("t", 0), ("q", 0), ("t", 1), ("q", 1), ("k", 0), ("k", 1))
    items = [(g, i) for g, (kind, _) in enumerate(GROUP) for i in range(4 if kind == "t" else 8)]
    cost = [0.25 if GROUP[g][0] == "t" else 1.0 for g, _ in items]
    parts = [[] for _ in range(UPP)]
    for n, item in enumerate(items):
        parts[min(UPP - 1, int(sum(cost[:n]) * UPP / sum(cost)))].append(item)
    ends = [[g for g, i in part if i == (3 if GROUP[g][0] == "t" else 7)] for part in parts]
    ctx = ExitStack()
    with ctx:
        sb = opener(ctx)
        w = sb("w_qkv", [P, 2, KD, 3, P])
        qT = sb("qT", [P, 2, SEQ])
        kT = sb("kT", [P, 2, SEQ])
        vT = sb("vT", [P, SEQ])
        V = sb("V", [P, 2, TT, P])
        bias = sb("bias", [P, 2, SLOTS, GRID_W])
        colmask = sb("colmask", [P, GRID_W])
        S = sb("S", [P, 2, SPAN])
        Pr = sb("Pr", [P, 2, SPAN])
        PT = sb("PT", [P, 2, 5, P])
        nmax = sb("nmax", [P, 2])
        rsum = sb("rsum", [P, 2])
        rinv = sb("rinv", [P, 2])
        O = sb("O", [P, 2, TT, P])
        ps_s = [banks(ctx, f"ps_s{i}", 2) for i in range(2)]
        ps_p = banks(ctx, "ps_p", 2)
        ps_o = ps_p[:, HALF + 2 * P:HALF + 2 * P + HEADDIM]
        ps_j = [banks(ctx, f"ps_j{i}", 1) for i in range(2)]

        s_w = [sem("c_w0"), sem("c_w1")]
        s_bias = [sem("c_bias0"), sem("c_bias1")]
        s_out = [sem("c_out0"), sem("c_out1")]
        mask_zero, mask_done, bias_done = sem("c_mz"), sem("c_md"), sem("c_bd")
        qk_done, max_done, exp_done, pt_mm, pt_ev, pv_done, o_done = (
            sem("c_qk"), sem("c_max"), sem("c_exp"), sem("c_ptmm"), sem("c_ptev"), sem("c_pv"), sem("c_o"))
        pt_ev2, rinv_done = sem("c_ptev2"), sem("c_rinv")
        proj_mm, proj_ev, chain = sem("c_projmm"), sem("c_projev"), sem("c_chain")

        def groups_before(p):
            return p * len(GROUP)

        with nc.Block() as block:
            @block.sync
            def _(sp):
                def load_w(p):
                    for part in range(3):
                        sp.dma_start(w[:, p % 2, :, part, :],
                                     w_in[:, :, COL_QKV + part * DM + p * P:COL_QKV + part * DM + (p + 1) * P]).then_inc(s_w[p % 2], 16)

                def load_bias(h):
                    for r in range(2):
                        src = rpb_scr[h, 1 - r:1 - r + SLOTS, :, :].rearrange("s q k -> q s k")
                        sp.dma_start(bias[r * GRID_W:(r + 1) * GRID_W, h % 2, :, :], src).then_inc(s_bias[h % 2], 16)

                load_w(0)
                load_bias(0)
                load_w(1)
                load_bias(1)
                for p in range(PAIRS):
                    for hh in range(2):
                        if 2 * p + hh + 2 < NA_HEADS:
                            sp.wait_ge(max_done, (2 * p + hh + 1) * TT)
                            load_bias(2 * p + hh + 2)
                    if p + 2 < PAIRS:
                        sp.wait_ge(proj_mm, groups_before(p + 1))
                        load_w(p + 2)
                    sp.wait_ge(o_done, (p + 1) * UPP)
                    sp.dma_start(na_scr[:, p * P:(p + 1) * P].rearrange("(t q) n -> q t n", q=P), O[:, p % 2, :, :]).then_inc(s_out[p % 2], 16)
                for i in range(2):
                    sp.wait_ge(s_out[i], 16 * (PAIRS // 2))

            @block.gpsimd
            def _(pool):
                nc.gpsimd.memset(colmask[:, :], 0.0).then_inc(mask_zero, 1)
                pool.wait_ge(mask_zero, 1)
                edge = GRID_W - NA_KW
                for r in range(2):
                    m = colmask[r * GRID_W:(r + 1) * GRID_W, :]
                    nc.gpsimd.affine_select(out=m[:, 0:edge], in_=m[:, 0:edge], compare_op=ALU.is_ge, fill=MASKED,
                                            base=NA_KW // 2, pattern=[[1, edge]], channel_multiplier=-1).then_inc(mask_zero, 1)
                    pool.wait_ge(mask_zero, 2 + r)
                    nc.gpsimd.affine_select(out=m[:, NA_KW:], in_=m[:, NA_KW:], compare_op=ALU.is_ge, fill=MASKED,
                                            base=NA_KW // 2 - 1 - NA_KW, pattern=[[-1, edge]], channel_multiplier=1).then_inc(mask_done, 1)
                pool.wait_ge(mask_done, 2)
                for h in range(NA_HEADS):
                    pool.wait_ge(s_bias[h % 2], 32 * (h // 2 + 1))
                    nc.gpsimd.tensor_tensor(bias[:, h % 2, :, :], bias[:, h % 2, :, :],
                                            colmask[:, :].unsqueeze(1).broadcast_to([P, SLOTS, GRID_W]), ALU.add).then_inc(bias_done, 1)

            @block.scalar
            def _(act):
                def proj_evac(p, g):
                    kind, half = GROUP[g]
                    n = groups_before(p) + g
                    act.wait_ge(proj_mm, n + 1)
                    if kind == "t":
                        dst, src = V[:, p % 2, 4 * half:4 * half + 4, :], ps_j[n % 2][:, :].rearrange("p (t n) -> p t n", t=4)
                    else:
                        whole = dict(q=qT[:, p % 2, :], k=kT[:, p % 2, :], v=vT[:, :])[kind]
                        dst, src = whole[:, half * HALF:(half + 1) * HALF], ps_j[n % 2][:, :]
                    nc.scalar.activation(dst, src, ACT.Copy).then_inc(proj_ev, 1)

                def probs_evac(u):
                    j = u % TT
                    act.wait_ge(pt_mm, u + 1)
                    if u >= 2:
                        act.wait_ge(pv_done, u - 1)
                    nc.scalar.activation(PT[:, u % 2, 0:4, :], ps_p[:, 0:HALF].rearrange("p (b n) -> p b n", b=4), ACT.Copy).then_inc(pt_ev, 1)
                    if inner[j]:
                        nc.scalar.activation(PT[0:GRID_W, u % 2, 4, :], ps_p[0:GRID_W, HALF:HALF + P], ACT.Copy).then_inc(pt_ev2, 1)

                for g in range(8):
                    proj_evac(0, g)
                for u in range(UNITS + 1):
                    if u >= 1:
                        probs_evac(u - 1)
                    if u < UNITS:
                        act.wait_ge(max_done, u + 1)
                        if u >= 2:
                            act.wait_ge(pt_mm, u - 1)
                        n = width[u % TT]
                        nc.scalar.activation(Pr[:, u % 2, 0:n], S[:, u % 2, 0:n], ACT.Exp, bias=nmax[:, u % 2:u % 2 + 1],
                                             accum_out=rsum[:, u % 2:u % 2 + 1]).then_inc(exp_done, 1)
                        p, s = divmod(u, UPP)
                        if p + 1 < PAIRS:
                            for g in ends[s]:
                                proj_evac(p + 1, g)

            inner_before = lambda u: (u // TT) * sum(inner) + sum(inner[:u % TT])

            @block.vector
            def _(v):
                links = 0

                def scale_out(u):
                    p, s = divmod(u, UPP)
                    hh, j = divmod(s, TT)
                    v.wait_ge(exp_done, u + 1)
                    nc.vector.reciprocal(rinv[:, u % 2:u % 2 + 1], rsum[:, u % 2:u % 2 + 1]).then_inc(rinv_done, 1)
                    v.wait_ge(pv_done, u + 1)
                    v.wait_ge(rinv_done, u + 1)
                    if s == 0 and p >= 2:
                        v.wait_ge(s_out[p % 2], 16 * (p // 2))
                    nc.vector.tensor_scalar(O[:, p % 2, j, hh * HEADDIM:(hh + 1) * HEADDIM], ps_o,
                                            rinv[:, u % 2:u % 2 + 1], None, ALU.mult).then_inc(o_done, 1)

                for u in range(UNITS + 1):
                    if u < UNITS:
                        h, j = divmod(u, TT)
                        n = width[j]
                        if j == 0:
                            v.wait_ge(bias_done, h + 1)
                        v.wait_ge(qk_done, u + 1)
                        if u >= 2:
                            v.wait_ge(exp_done, u - 1)
                        nc.vector.scalar_tensor_tensor(
                            out=S[:, u % 2, 0:n], in0=ps_s[u % 2][:, 0:n], scalar=HEADDIM ** -0.5,
                            in1=bias[:, h % 2, slot0[j]:slot0[j] + n // GRID_W, :].rearrange("p s c -> p (s c)"),
                            op0=ALU.mult, op1=ALU.add).then_inc(chain, 1)
                        links += 1
                        v.wait_ge(chain, links)
                        if inner[j]:
                            nc.vector.memset(S[0:GRID_W, u % 2, n - GRID_W:n], MASKED)
                            nc.vector.memset(S[GRID_W:P, u % 2, 0:GRID_W], MASKED).then_inc(chain, 1)
                            links += 1
                            v.wait_ge(chain, links)
                        nc.vector.tensor_reduce(nmax[:, u % 2:u % 2 + 1], S[:, u % 2, 0:n], AX.X, ALU.max, negate=True).then_inc(max_done, 1)
                    if u >= 1:
                        scale_out(u - 1)

            @block.tensor
            def _(pe):
                def project(p, part):
                    for g, i in part:
                        kind, half = GROUP[g]
                        n = groups_before(p) + g
                        bank = ps_j[n % 2]
                        if g == 0 and i == 0:
                            pe.wait_ge(s_w[p % 2], 48 * (p // 2 + 1))
                        if i == 0:
                            if kind == "t":
                                pe.wait_ge(proj_ev, groups_before(p) + half + 1)
                            if n >= 2:
                                pe.wait_ge(proj_ev, n - 1)
                        if kind == "t":
                            t = 4 * half + i
                            last = nc.tensor.transpose(bank[:, i * P:(i + 1) * P], vT[:, t * P:(t + 1) * P], ident[:, :])
                            end = i == 3
                        else:
                            last = nc.tensor.matmul(bank[:, :], w[:, p % 2, i, "qkv".index(kind), :], n1T[:, i, half * HALF:(half + 1) * HALF],
                                                    start=(i == 0), stop=(i == KD - 1))
                            end = i == KD - 1
                        if end:
                            last.then_inc(proj_mm, 1)

                for part in parts:
                    project(0, part)
                for u in range(UNITS + 1):
                    if u < UNITS:
                        p, s = divmod(u, UPP)
                        hh, j = divmod(s, TT)
                        if s == 0:
                            pe.wait_ge(proj_ev, groups_before(p + 1))
                        if u >= 2:
                            pe.wait_ge(max_done, u - 1)
                        rows = slice(hh * HEADDIM, (hh + 1) * HEADDIM)
                        k0 = first_row[j] * GRID_W
                        last = nc.tensor.matmul(ps_s[u % 2][:, 0:HALF], qT[rows, p % 2, j * P:(j + 1) * P],
                                                kT[rows, p % 2, k0:k0 + HALF], start=True, stop=True)
                        if inner[j]:
                            last = nc.tensor.matmul(ps_s[u % 2][:, HALF:HALF + GRID_W], qT[rows, p % 2, j * P:(j + 1) * P],
                                                    kT[rows, p % 2, k0 + HALF:k0 + HALF + GRID_W], start=True, stop=True)
                        last.then_inc(qk_done, 1)
                    if u >= 1:
                        t = u - 1
                        j = t % TT
                        pe.wait_ge(exp_done, t + 1)
                        if t >= 1:
                            pe.wait_ge(pt_ev, t)
                            pe.wait_ge(pt_ev2, inner_before(t)) if inner_before(t) else None
                        if inner[j] and t >= 1:
                            pe.wait_ge(o_done, t)
                        for b in range(4):
                            last = nc.tensor.transpose(ps_p[:, b * P:(b + 1) * P], Pr[:, t % 2, b * P:(b + 1) * P], ident[:, :])
                        if inner[j]:
                            last = nc.tensor.transpose(ps_p[0:GRID_W, HALF:HALF + P], Pr[:, t % 2, HALF:HALF + GRID_W], ident[:, :])
                        last.then_inc(pt_mm, 1)
                    if u < UNITS:
                        p, s = divmod(u, UPP)
                        if p + 1 < PAIRS:
                            project(p + 1, parts[s])
                    if u >= 1:
                        t = u - 1
                        p, s = divmod(t, UPP)
                        hh, j = divmod(s, TT)
                        pe.wait_ge(pt_ev, t + 1)
                        if inner[j]:
                            pe.wait_ge(pt_ev2, inner_before(t) + 1)
                        if t >= 1:
                            pe.wait_ge(o_done, t)
                        b0 = first_row[j] // 2
                        for b in range(5 if inner[j] else 4):
                            keys = P if b < 4 else GRID_W
                            last = nc.tensor.matmul(ps_o, PT[0:keys, t % 2, b, :],
                                                    V[0:keys, p % 2, b0 + b, hh * HEADDIM:(hh + 1) * HEADDIM],
                                                    start=(b == 0), stop=(b == (4 if inner[j] else 3)))
                        last.then_inc(pv_done, 1)


def stage_ssd(nc, a, opener, banks, sem, consts, X, BT, CT, dt, dA, zg_scr, y_rstd):
    f32 = mybir.dt.float32
    ALU, ACT, AX = mybir.AluOpType, mybir.ActivationFunctionType, mybir.AxisListType
    ident, upto, since, after, before, ones = consts
    H, GP = SSD_HEADS, HPG * HEADDIM
    UNITS = TT * GROUPS
    TAB = TT * H
    ctx = ExitStack()
    with ctx:
        sb = opener(ctx)
        tabs = sb("tabs", [P, 6, TT, H])
        w_state = sb("w_state", [P, 2, TT, H])
        Bt = sb("Bt", [P, TT, GROUPS * STATE])
        back = sb("back", [P, TT, DM])
        fwd = sb("fwd", [P, 2, DM])
        d_skip = sb("d_skip", [P, H])
        xb_state = sb("xb_state", [P, 2, DM])
        tmp = sb("tmpD", [P, DM])
        x_dt = sb("x_dt", [P, 2, 2, DM])
        xf_state = sb("xf_state", [P, DM])
        rhs = sb("rhsD", [P, 2, 2, HPG, P])
        E = sb("E", [P, 2, HPG, P])
        cb = sb("cb", [P, 2, P])
        M = sb("M", [P, 2, 2, HPG, P])
        off = sb("off", [P, 2, GP])
        skip = sb("skip", [P, GP])
        Y = sb("Y", [P, DM])
        z = sb("z", [P, 2, DM])
        sumsq = sb("sumsqD", [P, TT])
        ps_a = [banks(ctx, f"ps_a{i}", 1) for i in range(2)]
        ps_cb = banks(ctx, "ps_cb", 1)
        ps_y = [banks(ctx, f"ps_y{i}", 1) for i in range(2)]
        ps_off = banks(ctx, "ps_off", 1)
        ps_st = banks(ctx, "ps_st", 2)

        s_skip, tab_mm, tab_exp, w_done = sem("d_skip"), sem("d_tabmm"), sem("d_tabexp"), sem("d_w")
        s_z = [sem("d_z0"), sem("d_z1")]
        bt_mm, bt_ev = sem("d_btmm"), sem("d_btev")
        xb_done, bst_mm, bst_done, zero_done = sem("d_xb"), sem("d_bstmm"), sem("d_bst"), sem("d_zero")
        rhs_done, a_mm, e_done, cb_mm, m_done, y_mm, y_done = (
            sem("d_rhs"), sem("d_amm"), sem("d_e"), sem("d_cbmm"), sem("d_m"), sem("d_ymm"), sem("d_y"))
        cb_read, off_mm, off_read, xdt_done, xf_done, fst_mm, fwd_done, chain, gated, bchain = (
            sem("d_cbread"), sem("d_offmm"), sem("d_offread"), sem("d_xdt"), sem("d_xf"), sem("d_fstmm"),
            sem("d_fwd"), sem("d_chain"), sem("d_gated"), sem("d_bchain"))
        sq_done, rs_done = sem("d_sq"), sem("d_rs")

        def by_head(t, n=H, w=HEADDIM):
            return t.unsqueeze(2).broadcast_to([P, n, w])

        def heads(t):
            return t.rearrange("p (h e) -> p h e", e=HEADDIM)

        with nc.Block() as block:
            @block.sync
            def _(sp):
                sp.dma_start(d_skip[:, :], a["d_skip"][0].partition_broadcast(P)).then_inc(s_skip, 16)
                for c in range(TT):
                    if c >= 2:
                        sp.wait_ge(gated, c - 1)
                    sp.dma_start(z[:, c % 2, :], zg_scr[0, c * P:(c + 1) * P, :]).then_inc(s_z[c % 2], 16)

            @block.gpsimd
            def _(pool):
                nc.gpsimd.memset(back[:, TT - 1, :], 0.0).then_inc(zero_done, 1)
                nc.gpsimd.memset(fwd[:, 0, :], 0.0).then_inc(zero_done, 1)

                def build_rhs(u):
                    c, g = divmod(u, GROUPS)
                    if u >= 2:
                        pool.wait_ge(a_mm, u - 1)
                    for d, mask in ((0, upto), (1, since)):
                        nc.gpsimd.tensor_tensor(rhs[:, u % 2, d, :, :], mask[:, :].unsqueeze(1).broadcast_to([P, HPG, P]),
                                                dA[:, c, d * H + g * HPG:d * H + (g + 1) * HPG].unsqueeze(2).broadcast_to([P, HPG, P]),
                                                ALU.mult).then_inc(rhs_done, 1)

                def scale_x(c):
                    if c >= 2:
                        pool.wait_ge(y_mm, (c - 1) * GROUPS)
                    for d in range(2):
                        nc.gpsimd.tensor_tensor(heads(x_dt[:, c % 2, d, :]), heads(X[:, c, :]), by_head(dt[:, c, d * H:(d + 1) * H]),
                                                ALU.mult).then_inc(xdt_done, 1)

                def scale_for_state(c):
                    if c < TT - 1:
                        pool.wait_ge(w_done, 2)
                        if c >= 1:
                            pool.wait_ge(fst_mm, c)
                        nc.gpsimd.tensor_tensor(heads(xf_state[:, :]), heads(X[:, c, :]), by_head(w_state[:, 0, c, :]),
                                                ALU.mult).then_inc(xf_done, 1)

                scale_x(0)
                build_rhs(0)
                build_rhs(1)
                scale_for_state(0)
                for u in range(UNITS):
                    if u % GROUPS == 1 and u // GROUPS + 1 < TT:
                        scale_x(u // GROUPS + 1)
                    if u + 2 < UNITS:
                        build_rhs(u + 2)
                    if u % GROUPS == GROUPS - 1:
                        scale_for_state(u // GROUPS + 1)

            @block.scalar
            def _(act):
                act.wait_ge(tab_mm, 1)
                nc.scalar.activation(tabs[:, 0:4, :, :].rearrange("p k c h -> p (k c h)"), ps_a[0][:, :], ACT.Exp).then_inc(tab_exp, 1)
                nc.scalar.activation(tabs[:, 4:6, :, :].rearrange("p k c h -> p (k c h)"), ps_a[1][:, 0:2 * TAB], ACT.Exp).then_inc(tab_exp, 1)
                for c in range(TT):
                    act.wait_ge(bt_mm, c + 1)
                    nc.scalar.activation(Bt[:, c, :], ps_y[c % 2][:, :], ACT.Copy).then_inc(bt_ev, 1)
                for u in range(UNITS):
                    act.wait_ge(a_mm, u + 1)
                    if u >= 2:
                        act.wait_ge(m_done, 2 * (u - 1))
                    nc.scalar.activation(E[:, u % 2, :, :].rearrange("p h l -> p (h l)"), ps_a[u % 2][:, :], ACT.Exp).then_inc(e_done, 1)
                act.wait_ge(rs_done, 1)
                nc.scalar.activation(y_rstd[:, :], y_rstd[:, :], ACT.Sqrt).then_inc(sq_done, 1)

            @block.vector
            def _(v):
                v.wait_ge(tab_exp, 2)
                for d in range(2):
                    nc.vector.tensor_tensor(w_state[:, d, :, :], tabs[:, 2 + d, :, :], dt[:, :, d * H:(d + 1) * H], ALU.mult).then_inc(w_done, 1)
                v.wait_ge(w_done, 2)

                def scale_xb(n):
                    c = TT - 1 - n
                    if n >= 2:
                        v.wait_ge(bst_mm, n - 1)
                    nc.vector.tensor_tensor(heads(xb_state[:, n % 2, :]), heads(X[:, c, :]), by_head(w_state[:, 1, c, :]), ALU.mult).then_inc(xb_done, 1)

                scale_xb(0)
                v.wait_ge(zero_done, 2)
                for n in range(TT - 1):
                    c = TT - 1 - n
                    if n + 1 < TT - 1:
                        scale_xb(n + 1)
                    if n:
                        v.wait_ge(bst_done, n)
                    nc.vector.tensor_tensor(heads(tmp[:, :]), heads(back[:, c, :]), by_head(tabs[:, 5, c, :]), ALU.mult).then_inc(bchain, 1)
                    v.wait_ge(bchain, n + 1)
                    v.wait_ge(bst_mm, n + 1)
                    nc.vector.tensor_tensor(back[:, c - 1, :], tmp[:, :], ps_st[:, :], ALU.add).then_inc(bst_done, 1)
                v.wait_ge(bst_done, TT - 1)
                v.wait_ge(s_skip, 16)

                links = 0
                for u in range(UNITS + 1):
                    if u < UNITS:
                        c, g = divmod(u, GROUPS)
                        v.wait_ge(cb_mm, u + 1)
                        if u >= 1:
                            v.wait_ge(m_done, 2 * u)
                        for d, mask in ((0, upto), (1, since)):
                            nc.vector.tensor_tensor(cb[:, d, :], ps_cb[:, 0:P], mask[:, :], ALU.mult).then_inc(cb_read, 1)
                        v.wait_ge(cb_read, 2 * u + 2)
                        v.wait_ge(e_done, u + 1)
                        if u >= 2:
                            v.wait_ge(y_mm, u - 1)
                        for d in range(2):
                            nc.vector.tensor_tensor(M[:, u % 2, d, :, :], E[:, u % 2, :, :],
                                                    cb[:, d, :].unsqueeze(1).broadcast_to([P, HPG, P]), ALU.mult).then_inc(m_done, 1)
                    if u >= 1:
                        w = u - 1
                        c, g = divmod(w, GROUPS)
                        cols = slice(g * GP, (g + 1) * GP)
                        v.wait_ge(off_mm, w + 1)
                        if w:
                            v.wait_ge(y_done, w)
                        for d in range(2):
                            nc.vector.tensor_tensor(heads(off[:, d, :]), heads(ps_off[:, d * GP:(d + 1) * GP]),
                                                    by_head(tabs[:, d, c, g * HPG:(g + 1) * HPG], HPG), ALU.mult).then_inc(off_read, 1)
                        nc.vector.tensor_tensor(heads(skip[:, :]), heads(X[:, c, cols]), by_head(d_skip[:, g * HPG:(g + 1) * HPG], HPG),
                                                ALU.mult).then_inc(chain, 1)
                        v.wait_ge(off_read, 2 * w + 2)
                        nc.vector.tensor_tensor(off[:, 0, :], off[:, 0, :], off[:, 1, :], ALU.add).then_inc(chain, 1)
                        v.wait_ge(chain, links + 2)
                        nc.vector.tensor_tensor(off[:, 0, :], off[:, 0, :], skip[:, :], ALU.add).then_inc(chain, 1)
                        links += 3
                        v.wait_ge(chain, links)
                        v.wait_ge(y_mm, w + 1)
                        if g == 0 and c:
                            v.wait_ge(gated, c)
                        nc.vector.tensor_tensor(Y[:, cols], off[:, 0, :], ps_y[w % 2][:, 0:GP], ALU.add).then_inc(y_done, 1)
                        if g == GROUPS - 1:
                            if c < TT - 1:
                                if c:
                                    v.wait_ge(fwd_done, c)
                                nc.vector.tensor_tensor(heads(tmp[:, :]), heads(fwd[:, c % 2, :]), by_head(tabs[:, 4, c, :]), ALU.mult).then_inc(chain, 1)
                                links += 1
                                v.wait_ge(chain, links)
                                v.wait_ge(fst_mm, c + 1)
                                nc.vector.tensor_tensor(fwd[:, (c + 1) % 2, :], tmp[:, :], ps_st[:, :], ALU.add).then_inc(fwd_done, 1)
                            v.wait_ge(s_z[c % 2], 16 * (c // 2 + 1))
                            v.wait_ge(y_done, w + 1)
                            v.wait_ge(xdt_done, 2 * (c + 1))
                            v.wait_ge(xf_done, min(c + 1, TT - 1))
                            if c == TT - 1:
                                v.wait_ge(chain, links)
                            nc.vector.tensor_tensor(X[:, c, :], Y[:, :], z[:, c % 2, :], ALU.mult).then_inc(gated, 1)
                            v.wait_ge(gated, c + 1)
                            nc.vector.tensor_tensor_reduce(out=tmp[:, :], in0=X[:, c, :], in1=X[:, c, :], scale=1.0, scalar=0.0,
                                                           op0=ALU.mult, op1=ALU.add, accum_out=sumsq[:, c:c + 1]).then_inc(chain, 1)
                            links += 1
                            v.wait_ge(chain, links)
                nc.vector.tensor_scalar(y_rstd[:, :], sumsq[:, :], 1.0 / DM, EPS, ALU.mult, ALU.add).then_inc(rs_done, 1)
                v.wait_ge(sq_done, 1)
                nc.vector.reciprocal(y_rstd[:, :], y_rstd[:, :]).then_inc(rs_done, 1)

            @block.tensor
            def _(pe):
                for i, (mat, d) in enumerate(((upto, 0), (since, 1), (after, 0), (before, 1))):
                    nc.tensor.matmul(ps_a[0][:, i * TAB:(i + 1) * TAB], mat[:, :], dA[:, :, d * H:(d + 1) * H], start=True, stop=True)
                for d in range(2):
                    last = nc.tensor.matmul(ps_a[1][:, d * TAB:(d + 1) * TAB], ones[:, :], dA[:, :, d * H:(d + 1) * H], start=True, stop=True)
                last.then_inc(tab_mm, 1)
                for c in range(TT):
                    if c >= 2:
                        pe.wait_ge(bt_ev, c - 1)
                    for g in range(GROUPS):
                        last = nc.tensor.transpose(ps_y[c % 2][:, g * STATE:(g + 1) * STATE], BT[:, g, c * P:(c + 1) * P], ident[:, :])
                    last.then_inc(bt_mm, 1)

                def states(c, x_src, done):
                    for g in range(GROUPS):
                        last = nc.tensor.matmul(ps_st[:, g * GP:(g + 1) * GP], Bt[:, c, g * STATE:(g + 1) * STATE],
                                                x_src[:, g * GP:(g + 1) * GP], start=True, stop=True)
                    last.then_inc(done, 1)

                pe.wait_ge(bt_ev, TT)
                for n in range(TT - 1):
                    pe.wait_ge(xb_done, n + 1)
                    if n:
                        pe.wait_ge(bst_done, n)
                    states(TT - 1 - n, xb_state[:, n % 2, :], bst_mm)
                pe.wait_ge(tab_exp, 2)

                def decays(u):
                    pe.wait_ge(rhs_done, 2 * u + 2)
                    if u >= 2:
                        pe.wait_ge(e_done, u - 1)
                    nc.tensor.matmul(ps_a[u % 2][:, :], after[:, :], rhs[:, u % 2, 0, :, :].rearrange("p h l -> p (h l)"), start=True, stop=False)
                    nc.tensor.matmul(ps_a[u % 2][:, :], before[:, :], rhs[:, u % 2, 1, :, :].rearrange("p h l -> p (h l)"),
                                     start=False, stop=True).then_inc(a_mm, 1)

                def scores(u):
                    c, g = divmod(u, GROUPS)
                    if u:
                        pe.wait_ge(cb_read, 2 * u)
                    nc.tensor.matmul(ps_cb[:, 0:P], BT[:, g, c * P:(c + 1) * P], CT[:, g, c * P:(c + 1) * P],
                                     start=True, stop=True).then_inc(cb_mm, 1)

                decays(0)
                scores(0)
                pe.wait_ge(bst_done, TT - 1)
                for u in range(UNITS):
                    c, g = divmod(u, GROUPS)
                    if u + 1 < UNITS:
                        decays(u + 1)
                        scores(u + 1)
                    if g == 0:
                        pe.wait_ge(fwd_done, c) if c else pe.wait_ge(zero_done, 2)
                    if u:
                        pe.wait_ge(off_read, 2 * u)
                    cols = slice(g * GP, (g + 1) * GP)
                    for d, state in ((0, fwd[:, c % 2, cols]), (1, back[:, c, cols])):
                        last = nc.tensor.matmul(ps_off[:, d * GP:(d + 1) * GP], CT[:, g, c * P:(c + 1) * P], state, start=True, stop=True)
                    last.then_inc(off_mm, 1)
                    pe.wait_ge(m_done, 2 * u + 2)
                    pe.wait_ge(xdt_done, 2 * (c + 1))
                    if u >= 2:
                        pe.wait_ge(y_done, u - 1)
                    for h in range(HPG):
                        hc = slice(g * GP + h * HEADDIM, g * GP + (h + 1) * HEADDIM)
                        for d in range(2):
                            last = nc.tensor.matmul(ps_y[u % 2][:, h * HEADDIM:(h + 1) * HEADDIM], M[:, u % 2, d, h, :],
                                                    x_dt[:, c % 2, d, hc], start=(d == 0), stop=(d == 1))
                    last.then_inc(y_mm, 1)
                    if g == GROUPS - 2 and c < TT - 1:
                        pe.wait_ge(xf_done, c + 1)
                        if c:
                            pe.wait_ge(fwd_done, c)
                        states(c, xf_state, fst_mm)


def stage_merge(nc, a, opener, banks, sem, ident, X, y_rstd, zg_scr, na_scr, mix_scr):
    ALU, ACT = mybir.AluOpType, mybir.ActivationFunctionType
    ctx = ExitStack()
    with ctx:
        sb = opener(ctx)
        w_br = sb("w_br", [P, 2, KD, DM])
        g_rows = sb("g_rows", [KD, P])
        g_cols = sb("g_cols", [P, KD])
        RI = 3
        o_in = sb("o_in", [P, RI, DM])
        gates = sb("gates", [P, RI, 2, DM])
        yT = sb("yT", [P, 2, KD, P])
        oT = sb("oT", [P, 2, KD, P])
        mixed = sb("mixed", [P, 2, DM])
        side = sb("side", [P, DM])
        ps_t = [banks(ctx, f"ps_tE{i}", 2) for i in range(2)]
        ps_b = [banks(ctx, f"ps_bE{i}", 2) for i in range(2)]
        s_w = [[sem(f"e_w{i}{h}") for h in range(2)] for i in range(2)]
        s_g = sem("e_g")
        s_in = [sem(f"e_in{i}") for i in range(RI)]
        s_out = [sem("e_out0"), sem("e_out1")]
        g_mm, g_ev, t_mm, t_ev, b_mm, m_done, chain = (
            sem("e_gmm"), sem("e_gev"), sem("e_tmm"), sem("e_tev"), sem("e_bmm"), sem("e_m"), sem("e_chain"))

        with nc.Block() as block:
            @block.sync
            def _(sp):
                def load(t):
                    rows = slice(t * P, (t + 1) * P)
                    sp.dma_start(o_in[:, t % RI, :], na_scr[rows, :]).then_inc(s_in[t % RI], 16)
                    for i in range(2):
                        sp.dma_start(gates[:, t % RI, i, :], zg_scr[1 + i, rows, :]).then_inc(s_in[t % RI], 16)

                sp.dma_start(g_rows[:, :], a["ssd_norm_g"][0].rearrange("(k p) -> k p", p=P)).then_inc(s_g, 16)
                for i, name in enumerate(("w_ssd_br", "w_na_br")):
                    for h in range(2):
                        cols = slice(h * HALF, (h + 1) * HALF)
                        sp.dma_start(w_br[:, i, :, cols], a[name][0].rearrange("(k p) n -> p k n", p=P)[:, :, cols]).then_inc(s_w[i][h], 16)
                    if i == 0:
                        load(0)
                load(1)
                load(2)
                for t in range(TT):
                    sp.wait_ge(m_done, t + 1)
                    sp.dma_start(mix_scr[t * P:(t + 1) * P, :], mixed[:, t % 2, :]).then_inc(s_out[t % 2], 16)
                    if t + RI < TT:
                        load(t + RI)
                for i in range(2):
                    sp.wait_ge(s_out[i], 16 * (TT // 2))

            @block.scalar
            def _(act):
                act.wait_ge(g_mm, 1)
                nc.scalar.activation(g_cols[:, :], ps_b[0][:, 0:KD], ACT.Copy).then_inc(g_ev, 1)
                act.wait_ge(g_ev, 1)
                for t in range(TT):
                    act.wait_ge(t_mm, 2 * t + 1)
                    if t >= 2:
                        act.wait_ge(b_mm, 2 * (t - 2) + 1)
                    for k in range(KD):
                        last = nc.scalar.activation(yT[:, t % 2, k, :], ps_t[0][:, k * P:(k + 1) * P], ACT.Copy, scale=g_cols[:, k:k + 1])
                    last.then_inc(t_ev, 1)
                    act.wait_ge(t_mm, 2 * t + 2)
                    if t >= 2:
                        act.wait_ge(b_mm, 2 * (t - 2) + 2)
                    nc.scalar.activation(oT[:, t % 2, :, :], ps_t[1][:, :].rearrange("p (k n) -> p k n", k=KD), ACT.Copy).then_inc(t_ev, 1)

            @block.vector
            def _(v):
                links = 0
                for t in range(TT):
                    v.wait_ge(s_in[t % RI], 48 * (t // RI + 1))
                    v.wait_ge(b_mm, 2 * t + 1)
                    if t >= 2:
                        v.wait_ge(s_out[t % 2], 16 * (t // 2))
                    nc.vector.scalar_tensor_tensor(out=mixed[:, t % 2, :], in0=ps_b[0][:, :], scalar=y_rstd[:, t:t + 1],
                                                   in1=gates[:, t % RI, 0, :], op0=ALU.mult, op1=ALU.mult).then_inc(chain, 1)
                    v.wait_ge(b_mm, 2 * t + 2)
                    if t:
                        v.wait_ge(m_done, t)
                    nc.vector.tensor_tensor(side[:, :], ps_b[1][:, :], gates[:, t % RI, 1, :], ALU.mult).then_inc(chain, 1)
                    links += 2
                    v.wait_ge(chain, links)
                    nc.vector.tensor_tensor(mixed[:, t % 2, :], mixed[:, t % 2, :], side[:, :], ALU.add).then_inc(m_done, 1)

            @block.tensor
            def _(pe):
                pe.wait_ge(s_g, 16)
                nc.tensor.transpose(ps_b[0][:, 0:KD], g_rows[:, :], ident[0:KD, 0:KD]).then_inc(g_mm, 1)

                def turn(t):
                    pe.wait_ge(s_in[t % RI], 48 * (t // RI + 1))
                    for i, src in ((0, X[:, t, :]), (1, o_in[:, t % RI, :])):
                        if t:
                            pe.wait_ge(t_ev, 2 * (t - 1) + i + 1)
                        for k in range(KD):
                            last = nc.tensor.transpose(ps_t[i][:, k * P:(k + 1) * P], src[:, k * P:(k + 1) * P], ident[:, :])
                        last.then_inc(t_mm, 1)

                turn(0)
                pe.wait_ge(g_ev, 1)
                for t in range(TT):
                    if t + 1 < TT:
                        turn(t + 1)
                    for i, lhs in ((0, yT), (1, oT)):
                        pe.wait_ge(t_ev, 2 * t + i + 1)
                        if t:
                            pe.wait_ge(chain, 2 * (t - 1) + i + 1)
                        for h in range(2):
                            pe.wait_ge(s_w[i][h], 16)
                            for k in range(KD):
                                last = nc.tensor.matmul(ps_b[i][:, h * HALF:(h + 1) * HALF], lhs[:, t % 2, k, :],
                                                        w_br[:, i, k, h * HALF:(h + 1) * HALF], start=(k == 0), stop=(k == KD - 1))
                        last.then_inc(b_mm, 1)


def stage_peer(nc, a, opener, banks, sem, ident, mod_scr, mix_scr, out, s_out):
    f32, u32 = mybir.dt.float32, mybir.dt.uint32
    ALU, ACT, AX = mybir.AluOpType, mybir.ActivationFunctionType, mybir.AxisListType
    RU, RV, RD, RH, RI = 4, 4, 4, 3, 3
    ctx = ExitStack()
    with ctx:
        sb = opener(ctx)
        w_out = sb("w_out", [P, KD, DM])
        w_q = sb("w_q", [P, KD, QW])
        keys = sb("keys", [P, 2, P])
        keysT = sb("keysT", [P, 2, P])
        gate1 = sb("gate1", [P, DM])
        shift2 = sb("shift2", [P, DM])
        gain2 = sb("gain2", [P, DM])
        gate2 = sb("gate2", [P, DM])
        final_g = sb("final_g", [P, DM])
        h = sb("h", [P, RH, DM])
        n2 = sb("n2", [P, 2, DM])
        mixed = sb("mixedF", [P, DM])
        inT = sb("inT", [P, KD, P])
        qs = sb("qs", [P, QW])
        qT = sb("qT_F", [P, KD, P])
        junk = sb("junkF", [P, DM], mybir.dt.bfloat16)
        tmp = sb("tmpF", [P, DM])
        u_rows = sb("u_rows", [P, RU, DM])
        v_rows = sb("v_rows", [P, RV, DM])
        diag = sb("diag", [P, RD, P])
        stat = sb("stat", [P, 2])
        iota_i = sb("iota_i", [P, TOPK], u32)
        iota16 = sb("iota16", [P, TOPK])
        best = sb("best", [P, 2, TOPK])
        where = sb("where", [P, 2, TOPK], u32)
        where_f = sb("where_f", [P, 2, TOPK])
        rest = sb("rest", [P, NKEYS])
        cand = sb("cand", [P, TOPK, TOPK])
        cand2 = sb("cand2", [P, TOPK * TOPK])
        pos = sb("pos", [P, TOPK], u32)
        pos2 = sb("pos2", [P, 2, TOPK], u32)
        pos_f = sb("pos_f", [P, 2, TOPK])
        hit = sb("hit", [P, TOPK, TOPK])
        e_f = sb("e_f", [P, 2, TOPK])
        top = sb("top", [P, PEER_HEADS, TOPK])
        gates = sb("gatesF", [P, 2, PEER_HEADS, TOPK])
        gsum = sb("gsum", [P, 1])
        idx = sb("idx", [P, RI, PICKS], u32)
        dots = sb("dots", [P, PICKS])
        weight = sb("weight", [P, PICKS])
        acc = banks(ctx, "acc", 2)
        ps_A = banks(ctx, "ps_A", 2)
        ps_B = banks(ctx, "ps_B", 2)
        ps_C = banks(ctx, "ps_C", 2)

        s_wo, s_wq, s_keys, s_rows, s_mix = sem("f_wo"), sem("f_wq"), sem("f_keys"), sem("f_rows"), sem("f_mix")
        s_h = [sem(f"f_h{i}") for i in range(RH)]
        s_u = [sem(f"f_u{i}") for i in range(RU)]
        s_v = [sem(f"f_v{i}") for i in range(RV)]
        iota_done, iota_ready, gain_done, keys_mm, keys_ev = (
            sem("f_iota"), sem("f_iota16"), sem("f_gain"), sem("f_keysmm"), sem("f_keysev"))
        step_mm, step_ev, h_done, mean_done, root_done, n2_done, topk_done = (
            sem("f_step"), sem("f_ev"), sem("f_hd"), sem("f_mean"), sem("f_root"), sem("f_n2"), sem("f_topk"))
        u_used, v_used, diag_done, act_done, weight_done, shifted, exp_done = (
            sem("f_uused"), sem("f_vused"), sem("f_diag"), sem("f_act"), sem("f_weight"), sem("f_shift"), sem("f_exp"))
        acc_read, fin_mean, fin_root, fin_done, chain = (
            sem("f_accread"), sem("f_fmean"), sem("f_froot"), sem("f_fin"), sem("f_chain"))

        STEPS = ("mixT", "project", "n2T", "query0", "query1", "qT0", "score0", "qT1", "score1")
        BANKS = dict(mixT=ps_A, project=ps_B, n2T=ps_A, query0=ps_C, query1=ps_B, qT0=ps_A, score0=ps_C, qT1=ps_B, score1=ps_A)
        EVACS = tuple(s for s in STEPS if s != "project")
        PE_SLOT = dict(mixT=1, project=4, n2T=25, query0=29, query1=41, qT0=54, score0=57, qT1=60, score1=63)
        PART_SLOTS, PARTS = 3, 4
        H_SLOT, ROOT_SLOT, N_SLOT, TOPK_SLOT = 15, 18, 20, 62
        EXP_AT, GELU_AT, WEIGHT_AT = 1, 1, 3
        LAG = 24
        ROUTE_PARTS = 4
        PHASES = range(-1, TT + 1)

        def slots(i):
            return range(PICKS if i < TT else LAG + 5)

        def lagging(i, j):
            n = i * PICKS + j - LAG
            return (n, n // PICKS, n % PICKS) if 0 <= n < TT * PICKS else (None, None, None)

        def route_parts(i, j):
            parts = []
            if i == -1 and j >= TOPK_SLOT and j < TOPK_SLOT + ROUTE_PARTS:
                parts.append((0, 0, j - TOPK_SLOT))
            if i == 0 and j < ROUTE_PARTS * (PEER_HEADS - 1):
                parts.append((0, 1 + j // ROUTE_PARTS, j % ROUTE_PARTS))
            if 0 <= i < TT - 1 and j >= TOPK_SLOT and (j - TOPK_SLOT) % 2 == 0:
                part = (j - TOPK_SLOT) // 2
                if part < PEER_HEADS * ROUTE_PARTS:
                    parts.append((i + 1, part // ROUTE_PARTS, part % ROUTE_PARTS))
            return parts

        def exps(i, j):
            n = i * PICKS + j - EXP_AT
            return [(t, hd) for t, hd, part in route_parts(n // PICKS, n % PICKS) if part == ROUTE_PARTS - 1]

        def head_after(i, j, slots_after):
            n = i * PICKS + j - slots_after + 1
            if n > 0 and n % TOPK == 0 and n <= TT * PICKS:
                return divmod(n // TOPK - 1, PEER_HEADS)
            return None

        def steps_done(t, name):
            return len(STEPS) * t + STEPS.index(name) + 1

        def heads_done(t, hd):
            return PEER_HEADS * t + hd + 1

        def evacs_done(t, name):
            return len(EVACS) * t + EVACS.index(name) + 1

        with nc.Block() as block:
            @block.sync
            def _(sp):
                def load_mixed(t):
                    sp.dma_start(mixed[:, :], mix_scr[t * P:(t + 1) * P, :]).then_inc(s_mix, 16)

                def load_x(t):
                    sp.dma_start(h[:, t % RH, :], a["x"][0, t * P:(t + 1) * P, :]).then_inc(s_h[t % RH], 16)

                load_mixed(0)
                load_x(0)
                sp.dma_start(w_out[:, :, :], a["w_out"][0].rearrange("(k p) n -> p k n", p=P)).then_inc(s_wo, 16)
                for i, row in enumerate((gate1, shift2, gain2, gate2)):
                    sp.dma_start(row[:, :], mod_scr[(2 + i) * DM:(3 + i) * DM].partition_broadcast(P)).then_inc(s_rows, 16)
                sp.dma_start(tmp[:, :], a["norm2_g"][0].partition_broadcast(P)).then_inc(s_rows, 16)
                sp.dma_start(final_g[:, :], a["final_g"].partition_broadcast(P)).then_inc(s_rows, 16)
                sp.dma_start(keys[:, :, :], a["peer_keys"][0].rearrange("z n d -> n z d")).then_inc(s_keys, 16)
                sp.dma_start(w_q[:, :, :], a["peer_wq"][0].rearrange("(k p) n -> p k n", p=P)).then_inc(s_wq, 16)
                for i in PHASES:
                    t = i + 2
                    if t < TT:
                        sp.wait_ge(step_mm, steps_done(t - 1, "mixT"))
                        load_mixed(t)
                    if i >= 1:
                        sp.wait_ge(fin_done, i)
                        sp.dma_start(out[0, (i - 1) * P:i * P, :], tmp[:, :]).then_inc(s_out, 16)
                    if t < TT:
                        load_x(t)
                sp.wait_ge(s_out, 16 * TT)

            @block.gpsimd
            def _(pool):
                nc.gpsimd.iota(iota_i[:, :], pattern=[[1, TOPK]], base=0, channel_multiplier=0).then_inc(iota_done, 1)

                def gather(table, ring, r, t, j, done):
                    pool.indirect_dma_start(ring[:, r, :], None, table,
                                            bass.IndirectOffsetOnAxis(ap=idx[:, t % RI, j:j + 1], axis=0)).then_inc(done, 16)

                for i in range(TT + 1):
                    for j in slots(i):
                        n, tv, jv = lagging(i, j)
                        if n is not None:
                            if n >= RV:
                                pool.wait_ge(v_used, n - RV + 1)
                            gather(a["peer_v"][0], v_rows, n % RV, tv, jv, s_v[n % RV])
                        if i < TT:
                            if j % TOPK == 0:
                                pool.wait_ge(topk_done, heads_done(i, j // TOPK))
                            n = i * PICKS + j
                            if n >= RU:
                                pool.wait_ge(u_used, n - RU + 1)
                            gather(a["peer_u"][0], u_rows, n % RU, i, j, s_u[n % RU])

            @block.scalar
            def _(act):
                act.wait_ge(keys_mm, 1)
                nc.scalar.activation(keysT[:, :, :], ps_C[:, 0:2 * P].rearrange("p (z n) -> p z n", z=2), ACT.Copy).then_inc(keys_ev, 1)

                def evacuate(t, name):
                    act.wait_ge(step_mm, steps_done(t, name))
                    src = BANKS[name]
                    if name in ("mixT", "n2T"):
                        dst = inT[:, :, :].rearrange("p k n -> p (k n)")
                    elif name in ("qT0", "qT1"):
                        dst = qT[:, :, :].rearrange("p k n -> p (k n)")
                    else:
                        half = int(name[-1])
                        dst = qs[:, half * DM:(half + 1) * DM]
                        if name == "query0" and t:
                            act.wait_ge(topk_done, PEER_HEADS * t)
                    nc.scalar.activation(dst, src[:, :], ACT.Copy).then_inc(step_ev, 1)

                events = {PE_SLOT[s] + (PART_SLOTS * (PARTS - 1) + 2 if s in ("query0", "query1") else 2): s for s in EVACS}
                for i in PHASES:
                    t = i + 1
                    for j in slots(i):
                        for tr, hd in exps(i, j):
                            act.wait_ge(shifted, heads_done(tr, hd))
                            g = gates[:, tr % 2, hd, :]
                            nc.scalar.activation(g, g, ACT.Exp).then_inc(exp_done, 1)
                        after = head_after(i, j, GELU_AT)
                        if after:
                            tu, hd = after
                            act.wait_ge(u_used, tu * PICKS + (hd + 1) * TOPK)
                            d = dots[:, hd * TOPK:(hd + 1) * TOPK]
                            nc.scalar.activation(d, d, ACT.Gelu).then_inc(act_done, 1)
                        n, tv, jv = lagging(i, j)
                        if n is not None:
                            if jv % TOPK == 0:
                                act.wait_ge(weight_done, heads_done(tv, jv // TOPK))
                            if n >= RD:
                                act.wait_ge(v_used, n - RD + 1)
                            nc.scalar.activation(diag[:, n % RD, :], ident[:, :], ACT.Copy, scale=weight[:, jv:jv + 1]).then_inc(diag_done, 1)
                        if j == LAG + 2 and i >= 1:
                            act.wait_ge(fin_mean, i)
                            nc.scalar.activation(stat[:, 1:2], stat[:, 1:2], ACT.Sqrt).then_inc(fin_root, 1)
                        if t < TT:
                            if j in events:
                                evacuate(t, events[j])
                            if j == ROOT_SLOT:
                                act.wait_ge(mean_done, t + 1)
                                nc.scalar.activation(stat[:, 0:1], stat[:, 0:1], ACT.Sqrt).then_inc(root_done, 1)

            @block.vector
            def _(v):
                links = [0]

                def link(ins):
                    links[0] += 1
                    ins.then_inc(chain, 1)
                    v.wait_ge(chain, links[0])

                v.wait_ge(iota_done, 1)
                link(nc.vector.tensor_copy(iota16[:, :], iota_i[:, :]))
                v.wait_ge(s_rows, 96)
                link(nc.vector.scalar_tensor_tensor(out=gain2[:, :], in0=gain2[:, :], scalar=1.0, in1=tmp[:, :], op0=ALU.add, op1=ALU.mult))

                def residual(t):
                    ht = h[:, t % RH, :]
                    v.wait_ge(step_mm, steps_done(t, "project"))
                    link(nc.vector.tensor_tensor(n2[:, t % 2, :], ps_B[:, :], gate1[:, :], ALU.mult))
                    v.wait_ge(s_h[t % RH], 16 * (t // RH + 1))
                    nc.vector.tensor_tensor(ht, ht, n2[:, t % 2, :], ALU.add).then_inc(h_done, 1)
                    v.wait_ge(h_done, t + 1)
                    link(nc.vector.tensor_tensor_reduce(out=junk[:, :], in0=ht, in1=ht, scale=1.0, scalar=0.0, op0=ALU.mult, op1=ALU.add,
                                                        accum_out=stat[:, 0:1]))
                    nc.vector.tensor_scalar(stat[:, 0:1], stat[:, 0:1], 1.0 / DM, EPS, ALU.mult, ALU.add).then_inc(mean_done, 1)

                def second_norm(t):
                    v.wait_ge(root_done, t + 1)
                    link(nc.vector.reciprocal(stat[:, 0:1], stat[:, 0:1]))
                    link(nc.vector.scalar_tensor_tensor(out=n2[:, t % 2, :], in0=h[:, t % RH, :], scalar=stat[:, 0:1], in1=gain2[:, :],
                                                        op0=ALU.mult, op1=ALU.mult))
                    nc.vector.tensor_tensor(n2[:, t % 2, :], n2[:, t % 2, :], shift2[:, :], ALU.add).then_inc(n2_done, 1)
                    v.wait_ge(n2_done, t + 1)

                def top16(values, spare, val, ind):
                    link(nc.vector.max(val[:, 0:8], values))
                    link(nc.vector.max_index(ind[:, 0:8], val[:, 0:8], values))
                    link(nc.vector.match_replace(spare, val[:, 0:8], values, LOWEST))
                    link(nc.vector.max(val[:, 8:16], spare))
                    link(nc.vector.max_index(ind[:, 8:16], val[:, 8:16], spare))

                def route(t, hd, part):
                    if part < 2:
                        if hd % (PEER_HEADS // 2) == 0 and part == 0:
                            v.wait_ge(step_ev, evacs_done(t, "score0" if hd == 0 else "score1"))
                        b = 2 * hd + part
                        top16(qs[:, b * P:(b + 1) * P], rest[:, :], best[:, part, :], where[:, part, :])
                    elif part == 2:
                        best_pairs(hd)
                    else:
                        experts(t, hd)

                def best_pairs(hd):
                    link(nc.vector.tensor_copy(where_f[:, :, :], where[:, :, :]))
                    link(nc.vector.tensor_tensor(cand[:, :, :], best[:, 0, :].unsqueeze(2).broadcast_to([P, TOPK, TOPK]),
                                                 best[:, 1, :].unsqueeze(1).broadcast_to([P, TOPK, TOPK]), ALU.add))
                    top16(cand[:, :, :].rearrange("p a b -> p (a b)"), cand2[:, :], top[:, hd, :], pos[:, :])

                def experts(t, hd):
                    link(nc.vector.tensor_scalar(pos2[:, 0, :], pos[:, :], 4, None, ALU.logical_shift_right))
                    link(nc.vector.tensor_scalar(pos2[:, 1, :], pos[:, :], TOPK - 1, None, ALU.bitwise_and))
                    link(nc.vector.tensor_copy(pos_f[:, :, :], pos2[:, :, :]))
                    for z in range(2):
                        link(nc.vector.tensor_tensor(hit[:, :, :], iota16[:, :].unsqueeze(1).broadcast_to([P, TOPK, TOPK]),
                                                     pos_f[:, z, :].unsqueeze(2).broadcast_to([P, TOPK, TOPK]), ALU.is_equal))
                        link(nc.vector.tensor_tensor(hit[:, :, :], hit[:, :, :], where_f[:, z, :].unsqueeze(1).broadcast_to([P, TOPK, TOPK]),
                                                     ALU.mult))
                        link(nc.vector.tensor_reduce(e_f[:, z, :], hit[:, :, :], AX.X, ALU.add))
                    if t >= RI:
                        v.wait_ge(v_used, (t - RI + 1) * PICKS)
                    ins = nc.vector.scalar_tensor_tensor(out=idx[:, t % RI, hd * TOPK:(hd + 1) * TOPK], in0=e_f[:, 0, :],
                                                         scalar=float(NKEYS), in1=e_f[:, 1, :], op0=ALU.mult, op1=ALU.add)
                    ins.then_inc(topk_done, 1)
                    v.wait_ge(topk_done, heads_done(t, hd))
                    if t >= 2:
                        v.wait_ge(weight_done, heads_done(t - 2, hd))
                    nc.vector.tensor_tensor(gates[:, t % 2, hd, :], top[:, hd, :], top[:, hd, 0:1].broadcast_to([P, TOPK]),
                                            ALU.subtract).then_inc(shifted, 1)

                def weigh(t, hd):
                    g = gates[:, t % 2, hd, :]
                    picks = slice(hd * TOPK, (hd + 1) * TOPK)
                    v.wait_ge(exp_done, heads_done(t, hd))
                    link(nc.vector.tensor_reduce(gsum[:, :], g, AX.X, ALU.add))
                    link(nc.vector.reciprocal(gsum[:, :], gsum[:, :]))
                    v.wait_ge(act_done, heads_done(t, hd))
                    if t:
                        v.wait_ge(diag_done, (t - 1) * PICKS + (hd + 1) * TOPK)
                    nc.vector.scalar_tensor_tensor(out=weight[:, picks], in0=dots[:, picks], scalar=gsum[:, 0:1], in1=g,
                                                   op0=ALU.mult, op1=ALU.mult).then_inc(weight_done, 1)
                    v.wait_ge(weight_done, heads_done(t, hd))

                def finish_sum(t):
                    ht = h[:, t % RH, :]
                    v.wait_ge(v_used, (t + 1) * PICKS)
                    if t:
                        v.wait_ge(s_out, 16 * t)
                    nc.vector.tensor_tensor(tmp[:, :], acc[:, :], gate2[:, :], ALU.mult).then_inc(acc_read, 1)
                    v.wait_ge(acc_read, t + 1)
                    link(nc.vector.tensor_tensor(ht, ht, tmp[:, :], ALU.add))
                    link(nc.vector.tensor_tensor_reduce(out=junk[:, :], in0=ht, in1=ht, scale=1.0, scalar=0.0, op0=ALU.mult, op1=ALU.add,
                                                        accum_out=stat[:, 1:2]))
                    nc.vector.tensor_scalar(stat[:, 1:2], stat[:, 1:2], 1.0 / DM, EPS, ALU.mult, ALU.add).then_inc(fin_mean, 1)

                def finish_norm(t):
                    v.wait_ge(fin_root, t + 1)
                    link(nc.vector.reciprocal(stat[:, 1:2], stat[:, 1:2]))
                    nc.vector.scalar_tensor_tensor(out=tmp[:, :], in0=h[:, t % RH, :], scalar=stat[:, 1:2], in1=final_g[:, :],
                                                   op0=ALU.mult, op1=ALU.mult).then_inc(fin_done, 1)
                    v.wait_ge(fin_done, t + 1)

                for i in PHASES:
                    t = i + 1
                    for j in slots(i):
                        after = head_after(i, j, WEIGHT_AT)
                        if after:
                            weigh(*after)
                        if i >= 1 and j == LAG:
                            finish_sum(i - 1)
                        if i >= 1 and j == LAG + 4:
                            finish_norm(i - 1)
                        if 0 <= i < TT:
                            n = i * PICKS + j
                            v.wait_ge(s_u[n % RU], 16 * (n // RU + 1))
                            if n:
                                v.wait_ge(u_used, n)
                            nc.vector.tensor_tensor_reduce(out=junk[:, :], in0=u_rows[:, n % RU, :], in1=n2[:, i % 2, :], scale=1.0, scalar=0.0,
                                                           op0=ALU.mult, op1=ALU.add, accum_out=dots[:, j:j + 1]).then_inc(u_used, 1)
                        if t < TT:
                            if j in (H_SLOT, N_SLOT) and 0 <= i:
                                v.wait_ge(u_used, i * PICKS + j + 1)
                            if j == H_SLOT:
                                residual(t)
                            if j == N_SLOT:
                                second_norm(t)
                        for part in route_parts(i, j):
                            route(*part)

            @block.tensor
            def _(pe):
                pe.wait_ge(s_keys, 16)
                for z in range(2):
                    last = nc.tensor.transpose(ps_C[:, z * P:(z + 1) * P], keys[:, z, :], ident[:, :])
                last.then_inc(keys_mm, 1)
                pe.wait_ge(keys_ev, 1)

                def transposes(bank, src, t, name):
                    for k in range(KD):
                        last = nc.tensor.transpose(bank[:, k * P:(k + 1) * P], src[:, k * P:(k + 1) * P], ident[:, :])
                    last.then_inc(step_mm, 1)

                def columns(bank, part, w, c0):
                    half, ks = part // 2, part % 2
                    c0 += half * HALF
                    for k in range(ks * KD // 2, (ks + 1) * KD // 2):
                        last = nc.tensor.matmul(bank[:, half * HALF:(half + 1) * HALF], inT[:, k, :], w[:, k, c0:c0 + HALF],
                                                start=(k == 0), stop=(k == KD - 1))
                    if part == PARTS - 1:
                        last.then_inc(step_mm, 1)

                def run(t, name, part):
                    bank = BANKS[name]
                    if name == "mixT":
                        pe.wait_ge(s_mix, 16 * (t + 1))
                        if t:
                            pe.wait_ge(step_ev, evacs_done(t - 1, "score1"))
                        transposes(bank, mixed[:, :], t, name)
                    elif name == "project":
                        if part == 0:
                            pe.wait_ge(step_ev, evacs_done(t, "mixT"))
                            pe.wait_ge(s_wo, 16)
                        columns(bank, part, w_out, 0)
                    elif name == "n2T":
                        pe.wait_ge(n2_done, t + 1)
                        transposes(bank, n2[:, t % 2, :], t, name)
                    elif name in ("query0", "query1"):
                        if part == 0:
                            pe.wait_ge(step_ev, evacs_done(t, "n2T"))
                            pe.wait_ge(h_done, t + 1)
                            pe.wait_ge(s_wq, 16)
                        columns(bank, part, w_q, int(name[-1]) * DM)
                    elif name in ("qT0", "qT1"):
                        half = int(name[-1])
                        pe.wait_ge(step_ev, evacs_done(t, "query1" if half == 0 else "score0"))
                        transposes(bank, qs[:, half * DM:(half + 1) * DM], t, name)
                    else:
                        half = int(name[-1])
                        pe.wait_ge(step_ev, evacs_done(t, "qT0" if half == 0 else "qT1"))
                        for b in range(KD):
                            last = nc.tensor.matmul(bank[:, b * P:(b + 1) * P], qT[:, b, :], keysT[:, b % 2, :], start=True, stop=True)
                        last.then_inc(step_mm, 1)

                events = {}
                for s in STEPS:
                    events[PE_SLOT[s]] = (s, 0)
                    if s in ("project", "query0", "query1"):
                        events.update({PE_SLOT[s] + PART_SLOTS * part: (s, part) for part in range(PARTS)})
                for i in PHASES:
                    t = i + 1
                    for j in slots(i):
                        n, tv, jv = lagging(i, j)
                        if n is not None:
                            pe.wait_ge(s_v[n % RV], 16 * (n // RV + 1))
                            pe.wait_ge(diag_done, n + 1)
                            if jv == 0 and tv:
                                pe.wait_ge(acc_read, tv)
                            for half in range(2):
                                last = nc.tensor.matmul(acc[:, half * HALF:(half + 1) * HALF], diag[:, n % RD, :],
                                                        v_rows[:, n % RV, half * HALF:(half + 1) * HALF],
                                                        start=(jv == 0), stop=(jv == PICKS - 1))
                            last.then_inc(v_used, 1)
                        if t < TT and j in events:
                            run(t, *events[j])


_INS = ["x", "c", "w_ada", "b_ada", "norm1_g", "w_in", "conv_w", "conv_b", "dt_bias_f", "dt_bias_b", "a_log_f", "a_log_b",
        "d_skip", "ssd_norm_g", "w_ssd_br", "na_rpb", "w_na_br", "w_out", "norm2_g", "peer_wq", "peer_keys", "peer_u",
        "peer_v", "final_g"]


def kernel(**inputs):
    import concourse.bacc as bacc
    from concourse.bass_utils import run_bass_kernel_spmd

    nc = bacc.Bacc("TRN2", target_bir_lowering=False, num_devices=1)
    arrays, args = {}, {}
    for name in _INS:
        arr = np.ascontiguousarray(inputs[name])
        arrays[f"in_{name}"] = arr
        args[name] = nc.dram_tensor(f"in_{name}", arr.shape, mybir.dt.from_np(arr.dtype), kind="ExternalInput").ap()
    out = nc.dram_tensor("out", (1, SEQ, DM), mybir.dt.float32, kind="ExternalOutput").ap()
    build_program(nc, args, out)
    r = run_bass_kernel_spmd(nc, [arrays], core_ids=[0])
    return r.results[0]["out"]
```
